# Optimizing a Trainium2 kernel written in Bass

```python
import jax, jax.numpy as jnp
from jax import lax
import numpy as np

D_MODEL = 2048
BATCH = 1
SEQ = 256
DEPTH = 1

GRID_W = 64
CTX_LEN = 256
SSM_HEADS = 32
SSM_HEAD_DIM = 64
D_SSM = SSM_HEADS * SSM_HEAD_DIM
SSM_GROUPS = 8
D_STATE = 128
CONV_W = 5
CHUNK = 128
D_CONV_CH = D_SSM + 2 * SSM_GROUPS * D_STATE
ATTN_HEADS = 16
KV_HEADS = 4
HEAD_DIM = 128
D_ATTN = ATTN_HEADS * HEAD_DIM
D_KV = KV_HEADS * HEAD_DIM
ROPE_THETA = 10000.0
Q_BLOCK = 128
D_FF = -(-(8 * D_MODEL) // (3 * 256)) * 256
N_MOD = 6
EPS = 1e-6
PROJ_SIZES = (D_SSM, D_CONV_CH, 2 * SSM_HEADS, D_ATTN, D_KV, D_KV, 2 * D_MODEL)
D_IN = sum(PROJ_SIZES)

kernel_name = 'hybrid_ssd_gqa_prefix_dit_block'

def rms(t):
    tf = t.astype(jnp.float32)
    return (tf * lax.rsqrt(jnp.mean(tf * tf, axis=-1, keepdims=True) + EPS)).astype(t.dtype)

def modulate(h, shift, scale):
    return h * (1 + scale) + shift

def split_proj(p):
    idx = np.cumsum(PROJ_SIZES)[:-1].tolist()
    return jnp.split(p, idx, axis=-1)

def axial_rope_tables(rows, cols):
    n_freq = HEAD_DIM // 4
    inv = jnp.power(ROPE_THETA, -jnp.arange(n_freq, dtype=jnp.float32) / n_freq)
    ang = jnp.stack([rows.astype(jnp.float32)[:, None] * inv,
                     cols.astype(jnp.float32)[:, None] * inv], axis=1)
    return jnp.cos(ang), jnp.sin(ang)

def apply_rope(t, cos, sin):
    b, s, h, d = t.shape
    tr = t.reshape(b, s, h, 2, 2, d // 4)
    t1, t2 = tr[..., 0, :], tr[..., 1, :]
    cs = cos[None, :, None].astype(t.dtype)
    sn = sin[None, :, None].astype(t.dtype)
    return jnp.stack([t1 * cs - t2 * sn, t2 * cs + t1 * sn], axis=-2).reshape(b, s, h, d)

def dwconv(u, w, bias):
    pad = (CONV_W - 1) // 2
    out = lax.conv_general_dilated(u, w[:, None, :].astype(u.dtype), window_strides=(1,),
                                   padding=[(pad, pad)], dimension_numbers=('NWC', 'WIO', 'NWC'),
                                   feature_group_count=u.shape[-1])
    return out + bias.astype(u.dtype)

def ssd_prep(xbc, dt_raw, conv_w, conv_b, dt_bias):
    b, l, _ = xbc.shape
    xbc = jax.nn.silu(dwconv(xbc, conv_w, conv_b))
    gn = SSM_GROUPS * D_STATE
    xs = xbc[..., :D_SSM].reshape(b, l, SSM_HEADS, SSM_HEAD_DIM)
    bm = xbc[..., D_SSM:D_SSM + gn].reshape(b, l, SSM_GROUPS, D_STATE)
    cm = xbc[..., D_SSM + gn:].reshape(b, l, SSM_GROUPS, D_STATE)
    dt = jax.nn.softplus(dt_raw.reshape(b, l, 2, SSM_HEADS).astype(jnp.float32)
                         + dt_bias.astype(jnp.float32))
    return xs, bm, cm, dt

def ssd_scan(xs, dt, a_neg, bm, cm, h0):
    b, l, h, p = xs.shape
    g, n = bm.shape[2], bm.shape[3]
    nc = l // CHUNK
    f32 = jnp.float32
    rep = h // g
    bh = jnp.repeat(bm.astype(f32), rep, axis=2).reshape(b, nc, CHUNK, h, n)
    ch = jnp.repeat(cm.astype(f32), rep, axis=2).reshape(b, nc, CHUNK, h, n)
    xdt = (xs.astype(f32) * dt[..., None]).reshape(b, nc, CHUNK, h, p)
    a = (dt * a_neg).reshape(b, nc, CHUNK, h).transpose(0, 3, 1, 2)
    a_cum = jnp.cumsum(a, axis=-1)
    lower = jnp.tril(jnp.ones((CHUNK, CHUNK), dtype=bool))
    seg = jnp.exp(jnp.where(lower, a_cum[..., :, None] - a_cum[..., None, :], -jnp.inf))
    scores = jnp.einsum('bclhn,bcshn->bhcls', ch, bh) * seg
    y_diag = jnp.einsum('bhcls,bcshp->bclhp', scores, xdt)
    decay_to_end = jnp.exp(a_cum[..., -1:] - a_cum)
    chunk_states = jnp.einsum('bclhn,bhcl,bclhp->bchpn', bh, decay_to_end, xdt)
    chunk_decay = jnp.exp(a_cum[..., -1])

    def step(state, inp):
        dec, st = inp
        return dec[:, :, None, None] * state + st, state

    h_final, h_prev = lax.scan(step, h0.astype(f32),
                               (chunk_decay.transpose(2, 0, 1), chunk_states.transpose(1, 0, 2, 3, 4)))
    y_off = jnp.einsum('bclhn,cbhpn,bhcl->bclhp', ch, h_prev, jnp.exp(a_cum))
    return (y_diag + y_off).reshape(b, l, h, p), h_final

def bi_ssd(xs, bm, cm, dt, a_log, d_skip, h0_fwd, h0_bwd):
    a_neg = -jnp.exp(a_log.astype(jnp.float32))
    y_f, h_f = ssd_scan(xs, dt[:, :, 0], a_neg[0], bm, cm, h0_fwd)
    rev = lambda t: jnp.flip(t, axis=1)
    y_b, h_b = ssd_scan(rev(xs), rev(dt[:, :, 1]), a_neg[1], rev(bm), rev(cm), h0_bwd)
    y = y_f + rev(y_b) + d_skip.astype(jnp.float32)[:, None] * xs.astype(jnp.float32)
    return y.astype(xs.dtype), h_f, h_b

def ssm_output(y, z, norm_g):
    b, l = z.shape[:2]
    gsz = D_SSM // SSM_GROUPS
    gated = y.reshape(b, l, SSM_GROUPS, gsz) * jax.nn.silu(z).reshape(b, l, SSM_GROUPS, gsz)
    return rms(gated).reshape(b, l, D_SSM) * norm_g

def attend_blocks(q, keys, vals):
    b, s = q.shape[:2]
    nb = s // Q_BLOCK
    rep = ATTN_HEADS // KV_HEADS
    qb = q.reshape(b, nb, Q_BLOCK, KV_HEADS, rep, HEAD_DIM).transpose(1, 0, 2, 3, 4, 5)
    scale = HEAD_DIM ** -0.5

    def one_block(qi):
        sc = jnp.einsum('bqgrd,bkgd->bgrqk', qi, keys).astype(jnp.float32) * scale
        pr = jax.nn.softmax(sc, axis=-1).astype(vals.dtype)
        return jnp.einsum('bgrqk,bkgd->bqgrd', pr, vals)

    out = lax.map(one_block, qb)
    return out.transpose(1, 0, 2, 3, 4, 5).reshape(b, s, D_ATTN)

def branch_merge(gates, ssm_br, attn_br):
    g_ssm, g_attn = jnp.split(gates, 2, axis=-1)
    return jax.nn.sigmoid(g_ssm) * ssm_br + jax.nn.sigmoid(g_attn) * attn_br

def swiglu(h, w_in, w_out):
    gate, up = jnp.split(h @ w_in, 2, axis=-1)
    return (jax.nn.silu(gate) * up) @ w_out

def setup_inputs(seed: int = 0) -> dict:
    key = jax.random.key(seed)
    ks = jax.random.split(key, 24)
    f32 = jnp.float32

    def nrm(k, shape, fan_in, gain=1.0):
        return jax.random.normal(k, shape, f32) * (gain * fan_in ** -0.5)

    dt0 = jnp.exp(jax.random.uniform(ks[9], (DEPTH, 2, SSM_HEADS), f32,
                                     minval=float(np.log(1e-3)), maxval=float(np.log(1e-1))))
    dt_bias = dt0 + jnp.log(-jnp.expm1(-dt0))
    a_log = jnp.log(jax.random.uniform(ks[10], (DEPTH, 2, SSM_HEADS), f32, minval=1.0, maxval=16.0))
    return {
        'x': jax.random.normal(ks[0], (BATCH, SEQ, D_MODEL), f32),
        'c': jax.random.normal(ks[1], (BATCH, D_MODEL), f32),
        'ctx': jax.random.normal(ks[2], (BATCH, CTX_LEN, D_MODEL), f32),
        'c_ctx': jax.random.normal(ks[3], (D_MODEL,), f32),
        'w_mod': nrm(ks[4], (DEPTH, D_MODEL, N_MOD * D_MODEL), D_MODEL, 0.5),
        'b_mod': 0.02 * jax.random.normal(ks[5], (DEPTH, N_MOD * D_MODEL), f32),
        'norm1': 1.0 + 0.05 * jax.random.normal(ks[6], (DEPTH, D_MODEL), f32),
        'w_in': nrm(ks[7], (DEPTH, D_MODEL, D_IN), D_MODEL),
        'conv_w': nrm(ks[8], (DEPTH, CONV_W, D_CONV_CH), CONV_W),
        'conv_b': 0.02 * jax.random.normal(ks[11], (DEPTH, D_CONV_CH), f32),
        'dt_bias': dt_bias,
        'a_log': a_log,
        'd_skip': 1.0 + 0.1 * jax.random.normal(ks[12], (DEPTH, SSM_HEADS), f32),
        'ssm_norm': 1.0 + 0.05 * jax.random.normal(ks[13], (DEPTH, D_SSM), f32),
        'q_norm': 1.0 + 0.05 * jax.random.normal(ks[14], (DEPTH, HEAD_DIM), f32),
        'k_norm': 1.0 + 0.05 * jax.random.normal(ks[15], (DEPTH, HEAD_DIM), f32),
        'w_ssm_br': nrm(ks[16], (DEPTH, D_SSM, D_MODEL), D_SSM),
        'w_attn_br': nrm(ks[17], (DEPTH, D_ATTN, D_MODEL), D_ATTN),
        'w_o': nrm(ks[18], (DEPTH, D_MODEL, D_MODEL), D_MODEL),
        'norm2': 1.0 + 0.05 * jax.random.normal(ks[19], (DEPTH, D_MODEL), f32),
        'w_ffn_in': nrm(ks[20], (DEPTH, D_MODEL, 2 * D_FF), D_MODEL),
        'w_ffn_out': nrm(ks[21], (DEPTH, D_FF, D_MODEL), D_FF),
    }

def reference(x, c, ctx, c_ctx, w_mod, b_mod, norm1, w_in, conv_w, conv_b, dt_bias, a_log, d_skip,
              ssm_norm, q_norm, k_norm, w_ssm_br, w_attn_br, w_o, norm2, w_ffn_in, w_ffn_out):
    b, s, _ = x.shape
    n_ctx = ctx.shape[1]
    rows_n = s // GRID_W
    rows = jnp.repeat(jnp.arange(rows_n), GRID_W)
    cols = jnp.tile(jnp.arange(GRID_W), rows_n)
    cos, sin = axial_rope_tables(rows, cols)
    h0 = jnp.zeros((b, SSM_HEADS, SSM_HEAD_DIM, D_STATE), jnp.float32)

    for i in range(DEPTH):
        sh1, sc1, gt1, sh2, sc2, gt2 = [m[:, None, :] for m in
                                        jnp.split(jax.nn.silu(c) @ w_mod[i] + b_mod[i], N_MOD, axis=-1)]
        csh1, csc1, cgt1, csh2, csc2, cgt2 = [m[None, None, :] for m in
                                              jnp.split(jax.nn.silu(c_ctx) @ w_mod[i] + b_mod[i], N_MOD, axis=-1)]
        z_l, xbc_l, dtr_l, q_l, k_l, v_l, g_l = split_proj(modulate(rms(x) * norm1[i], sh1, sc1) @ w_in[i])
        z_c, xbc_c, dtr_c, q_c, k_c, v_c, g_c = split_proj(modulate(rms(ctx) * norm1[i], csh1, csc1) @ w_in[i])

        xs_c, bm_c, cm_c, dt_c = ssd_prep(xbc_c, dtr_c, conv_w[i], conv_b[i], dt_bias[i])
        xs_l, bm_l, cm_l, dt_l = ssd_prep(xbc_l, dtr_l, conv_w[i], conv_b[i], dt_bias[i])
        y_c, hf_c, hb_c = bi_ssd(xs_c, bm_c, cm_c, dt_c, a_log[i], d_skip[i], h0, h0)
        y_l, _, _ = bi_ssd(xs_l, bm_l, cm_l, dt_l, a_log[i], d_skip[i], hf_c, hb_c)
        ssm_br_l = ssm_output(y_l, z_l, ssm_norm[i]) @ w_ssm_br[i]

        ck = rms(k_c.reshape(b, n_ctx, KV_HEADS, HEAD_DIM)) * k_norm[i]
        cv = v_c.reshape(b, n_ctx, KV_HEADS, HEAD_DIM)
        ql = apply_rope(rms(q_l.reshape(b, s, ATTN_HEADS, HEAD_DIM)) * q_norm[i], cos, sin)
        kl = apply_rope(rms(k_l.reshape(b, s, KV_HEADS, HEAD_DIM)) * k_norm[i], cos, sin)
        vl = v_l.reshape(b, s, KV_HEADS, HEAD_DIM)
        keys = jnp.concatenate([ck, kl], axis=1)
        vals = jnp.concatenate([cv, vl], axis=1)
        attn_br_l = attend_blocks(ql, keys, vals) @ w_attn_br[i]

        x_mid = x + gt1 * (branch_merge(g_l, ssm_br_l, attn_br_l) @ w_o[i])
        x_new = x_mid + gt2 * swiglu(modulate(rms(x_mid) * norm2[i], sh2, sc2), w_ffn_in[i], w_ffn_out[i])

        if i < DEPTH - 1:
            ssm_br_c = ssm_output(y_c, z_c, ssm_norm[i]) @ w_ssm_br[i]
            qc = rms(q_c.reshape(b, n_ctx, ATTN_HEADS, HEAD_DIM)) * q_norm[i]
            attn_br_c = attend_blocks(qc, ck, cv) @ w_attn_br[i]
            ctx_mid = ctx + cgt1 * (branch_merge(g_c, ssm_br_c, attn_br_c) @ w_o[i])
            ctx = ctx_mid + cgt2 * swiglu(modulate(rms(ctx_mid) * norm2[i], csh2, csc2),
                                          w_ffn_in[i], w_ffn_out[i])
        x = x_new
    return x


_drawn_inputs = setup_inputs


def setup_inputs(seed=0):
    import zlib

    import numpy as np

    out = dict(_drawn_inputs(seed))
    spreads = {}
    factors = {'ctx': 3.717,
     'norm1': 4.533,
     'conv_b': 8.0,
     'd_skip': 8.0,
     'ssm_norm': 6.292,
     'q_norm': 8.0,
     'k_norm': 8.0,
     'norm2': 3.816}
    for name, (base, spread) in spreads.items():
        noise = np.random.default_rng([zlib.crc32(name.encode()), seed]).standard_normal(out[name].shape)
        drawn = base * np.exp(spread * noise) if base else spread * noise
        out[name] = __import__('jax').numpy.asarray(drawn.astype(out[name].dtype))
    for name, factor in factors.items():
        out[name] = (out[name] * factor).astype(out[name].dtype)
    return out
```

```python
from contextlib import ExitStack

import numpy as np

import concourse.bass as bass
from concourse import mybir

F32 = mybir.dt.float32
F32R = mybir.dt.float32r
ALU = mybir.AluOpType
ACT = mybir.ActivationFunctionType
AX_X = mybir.AxisListType.X

P = 128
D = 2048
T = 256
TT = T // P
KT = D // P
HEADS, HD = 32, 64
GROUPS, NST = 8, 128
HPG = HEADS // GROUPS
TAPS = 5
AH, KVH, AD = 16, 4, 128
REP = AH // KVH
DFF = 5632
FT = DFF // P
GRID_W, THETA = 64, 10000.0
EPS = 1e-6
CZ, CX, CB, CC, CDT = 0, 2048, 4096, 5120, 6144
CQ, CK, CV, CG = 6208, 8256, 8768, 9280
DIN = 13376
NB = 512
CK_T = 4
RAW, SPL = 4, 2


class Phase:

    def __init__(self, name, n, chunks, kind, tiles, banks, staged=False):
        self.name, self.n, self.chunks, self.kind = name, n, chunks, kind
        self.tiles, self.banks, self.staged = tiles, banks, staged


def plan(phases):
    raw_user = [None] * RAW
    spl_user = [None] * SPL
    loads = [0] * RAW
    count = {"mod": 0, "split": 0}
    banks = done = 0
    staged = [0] * 4
    for ph in phases:
        ph.loaded, ph.raw_prev, ph.index, ph.spl_prev = [], [], [], []
        ph.bank0, ph.done0, ph.stage0 = [], [], []
        for _ in range(ph.n):
            ph.bank0.append(banks)
            ph.done0.append(done)
            ph.stage0.append(list(staged))
            banks += len(ph.banks)
            done += len(ph.banks) - len(ph.banks) // max(1, len(ph.tiles))
            if ph.staged:
                for b in range(len(ph.banks)):
                    staged[b] += 16
            row = [[], [], [], []]
            for p in range(ph.chunks):
                s = p % RAW
                loads[s] += 1
                row[0].append(loads[s] * 16)
                row[1].append(raw_user[s])
                row[2].append(count[ph.kind])
                raw_user[s] = (ph.kind, count[ph.kind])
                if ph.kind == "split":
                    row[3].append(spl_user[p % SPL])
                    spl_user[p % SPL] = count["split"]
                else:
                    row[3].append(None)
                count[ph.kind] += 1
            for a, b in zip((ph.loaded, ph.raw_prev, ph.index, ph.spl_prev), row):
                a.append(b)
        ph.banks_end, ph.staged_end, ph.count_end = banks, list(staged), dict(count)


def lin(values, i):
    if isinstance(i, int):
        return values[i]
    step = values[2] - values[1]
    assert all(b - a == step for a, b in zip(values[1:], values[2:]))
    return i * step + (values[1] - step)


def each_block(eng, n, body):
    body(0)
    if n == 2:
        body(1)
    elif n > 2:
        with eng.Fori(1, n) as i:
            body(i)


def hybrid_block(nc, a, out):
    with ExitStack() as outer:
        def sem(name):
            return outer.enter_context(nc.semaphore(name))

        def sb(name, shape, dt=F32, scope=outer):
            return scope.enter_context(nc.sbuf_tensor(name, shape, dt))

        def dram(name, shape):
            return nc.dram_tensor(name, shape, F32, kind="Internal").ap()

        proj_lat, proj_ctx = dram("proj_lat", (T, DIN)), dram("proj_ctx", (T, DIN))
        y_dram, xmid_dram, gate2_dram = dram("y_scratch", (T, D)), dram("xmid", (T, D)), dram("gate2", (1, D))

        LAT, BOTH = [0, 1], [0, 1, 2, 3]
        p_mod = Phase("mod", 24, 4, "mod", [], [])
        p_kv = Phase("kv", 2, 4, "split", BOTH, BOTH, True)
        p_xb = Phase("xb", 6, 4, "split", BOTH, BOTH, True)
        p_dt = Phase("dt", 1, 1, "split", BOTH, BOTH)
        p_q = Phase("q", 4, 4, "split", LAT, LAT, True)
        p_c = Phase("c", 2, 4, "split", LAT, LAT, True)
        p_z = Phase("z", 4, 4, "split", LAT, LAT, True)
        p_g = Phase("g", 8, 4, "split", LAT, LAT, True)
        p_br = Phase("br", 4, 8, "split", LAT, BOTH)
        p_o = Phase("o", 4, 4, "split", LAT, LAT)
        p_f1 = Phase("f1", DFF // NB, 8, "split", LAT, BOTH)
        p_f2 = Phase("f2", 4, FT // CK_T, "split", LAT, LAT)
        phases = [p_mod, p_kv, p_xb, p_dt, p_q, p_c, p_z, p_g, p_br, p_o, p_f1, p_f2]
        plan(phases)
        PROJ_COL = {"kv": CK, "xb": CX, "q": CQ, "c": CC, "z": CZ, "g": CG}

        def kview(w):
            return w.rearrange("(c k p) n -> c p k n", p=P, k=CK_T)

        w_mod, w_in = kview(a["w_mod"][0]), kview(a["w_in"][0])
        w_sb, w_ab, w_ob = kview(a["w_ssm_br"][0]), kview(a["w_attn_br"][0]), kview(a["w_o"][0])
        w_f1, w_f2 = kview(a["w_ffn_in"][0]), kview(a["w_ffn_out"][0])
        w_dt = a["w_in"][0].rearrange("(k p) n -> p k n", p=P)[:, :, CDT:CDT + 64]
        x_in = a["x"][0].rearrange("(t p) n -> p t n", p=P)
        ctx_in = a["ctx"][0].rearrange("(t p) n -> p t n", p=P)

        def source(ph, i, p):
            if ph is p_mod:
                return w_mod[p, :, :, bass.ts(i, NB)]
            if ph.name in PROJ_COL:
                return w_in[p, :, :, bass.ds(i * NB + PROJ_COL[ph.name], NB)]
            if ph is p_br:
                return (w_ab if p < 4 else w_sb)[p % 4, :, :, bass.ts(i, NB)]
            if ph is p_o:
                return w_ob[p, :, :, bass.ts(i, NB)]
            if ph is p_f1:
                return w_f1[p % 4, :, :, bass.ds(i * NB + (p // 4) * DFF, NB)]
            return w_f2[p, :, :, bass.ts(i, NB)]

        PS = outer.enter_context(nc.psum_tensor("PS", [P, 8, NB], F32))
        raw = sb("raw", [P, RAW, CK_T, NB])
        w_hi = sb("w_hi", [P, SPL, CK_T, NB], F32R)
        w_lo = sb("w_lo", [P, SPL, CK_T, NB], F32R)
        ident = sb("ident", [P, P])
        ones = sb("ones", [P, P])
        tri = sb("tri", [P, 2, P])
        mod = sb("mod", [P, 96, 2])
        b_col = sb("b_col", [P, 96])
        vec_col = sb("vec_col", [P, 80])
        conv_w = sb("conv_w", [P, TAPS * 32])
        s1 = sb("s1", [P, KT, 2])
        s2 = sb("s2", [P, KT])
        tmp = sb("tmp", [P, 2, 2, T])
        stage = sb("stage", [P, 4, NB])
        stat = sb("stat", [P, 16])
        dskip = sb("dskip", [P, HEADS])
        dtb = sb("dtb", [P, 64])
        aneg = sb("aneg", [P, 64])
        junk = stage[:, :, :].rearrange("p a b -> p (a b)")

        s_A = ExitStack()
        act1_hi = sb("act1_hi", [P, 32, T], F32R, s_A)
        act1_lo = sb("act1_lo", [P, 32, T], F32R, s_A)
        s_0 = ExitStack()
        x_tok = sb("x_tok", [P, 4, D], F32, s_0)
        rows = sb("rows", [P, 4, P], F32, s_0)
        c_rows = sb("c_rows", [32, P], F32, s_0)
        c_col = sb("c_col", [P, 2 * KT], F32, s_0)
        s_0.close()
        s_1 = ExitStack()
        dt = sb("dt", [P, 4, 64], F32, s_1)
        av = sb("av", [P, 4, 64], F32, s_1)
        acum = sb("acum", [P, 4, 64], F32, s_1)
        etot = sb("etot", [P, 4, 64], F32, s_1)
        eacum = sb("eacum", [P, 4, 64], F32, s_1)
        wdec = sb("wdec", [P, 4, 64], F32, s_1)
        s_2 = ExitStack()
        rope = sb("rope", [P, 2, 2, AD], F32, s_2)
        cos5 = sb("cos5", [P, 2, 5, AD], F32, s_2)
        sin5 = sb("sin5", [P, 2, 5, AD], F32, s_2)
        gain5 = sb("gain5", [P, 5, AD], F32, s_2)
        qk = sb("qk", [P, 12, AD], F32, s_2)
        qk_sq = sb("qk_sq", [P, 12, AD], F32, s_2)
        qk_r = sb("qk_r", [P, 10, AD], F32, s_2)
        vv = sb("vv", [P, 4, AD], F32, s_2)
        qT = sb("qT", [P, REP, T], F32, s_2)
        kT = sb("kT", [P, 2 * T], F32, s_2)
        probs = sb("probs", [P, 2, 2 * T], F32, s_2)
        pT = sb("pT", [P, 2, 4, T], F32, s_2)
        ast = sb("ast", [P, 64], F32, s_2)
        s_2.close()
        s_3 = ExitStack()
        negm = sb("negm", [P, 2, P], F32, s_3)
        a_loc = sb("a_loc", [P, 2, 2, HPG], F32, s_3)
        u_lat = sb("u_lat", [P, 2, 512], F32, s_3)
        u_ctx = sb("u_ctx", [P, 2, 384], F32, s_3)
        cin = sb("cin", [P, 7, T + 4], F32, s_3)
        cv = sb("cv", [P, 7, T], F32, s_3)
        tokb = sb("tokb", [P, 4, 384], F32, s_3)
        dec = sb("dec", [P, 4, HPG, P], F32, s_3)
        xdt = sb("xdt", [P, 2, 2, 256], F32, s_3)
        hst = sb("hst", [P, 2, 2, 256], F32, s_3)
        yb = sb("yb", [P, 2, 256], F32, s_3)
        zt = sb("zt", [P, 2, 256], F32, s_3)
        sst = sb("sst", [P, 8], F32, s_3)
        s_3.close()
        s_1.close()
        s_4 = ExitStack()
        wide = sb("wide", [P, 2, D], F32, s_4)
        gates = sb("gates", [P, 2, 2, NB], F32, s_4)
        xres = sb("xres", [P, 2, D], F32, s_4)
        gt1 = sb("gt1", [P, D], F32, s_4)
        diag = sb("diag", [P, 4, P], F32, s_4)
        s_4.close()
        s_A.close()
        act2_hi = sb("act2_hi", [P, 60, T], F32R)
        act2_lo = sb("act2_lo", [P, 60, T], F32R)
        H2 = FT
        xdf, xdb = cin[:, 0:3, 2:2 + T], cin[:, 3:6, 2:2 + T]
        yt = dec[:, :, :, :].rearrange("p c h l -> p (c h l)")[:, 0:1024].rearrange("p (c n) -> p c n", c=2)
        yx = cv[:, 4:6, :]

        setup_in, x_loaded, c_silu, vec_T, cols_ready = map(sem, (
            "setup_in", "x_loaded", "c_silu", "vec_T", "cols_ready"))
        raw_loaded = [sem(f"raw_loaded{s}") for s in range(RAW)]
        mod_used, mod_ready = sem("mod_used"), sem("mod_ready")
        hi_ready, lo_ready, pe_used = sem("hi_ready"), sem("lo_ready"), sem("pe_used")
        bank_done, bank_free = sem("bank_done"), sem("bank_free")
        stored = [sem(f"stored{s}") for s in range(4)]
        n_sq, n_sqrt, n_rec, n_mul = sem("n_sq"), sem("n_sqrt"), sem("n_rec"), sem("n_mul")
        tp_done, tp_tmp, tp_hi, tp_lo = sem("tp_done"), sem("tp_tmp"), sem("tp_hi"), sem("tp_lo")
        consts = sem("consts")
        d_dve, d_act, d_pe = sem("d_dve"), sem("d_act"), sem("d_pe")
        r_in, r_dve = sem("r_in"), sem("r_dve")
        (a_in, a_vin, a_dve, a_ssq, a_sqrt, a_rope, a_qkT, a_qkS, a_sc, a_max, a_exp, a_rec, a_norm, a_pT,
         a_pTs, a_pv, a_ohi, a_o) = map(sem, (
             "a_in", "a_vin", "a_dve", "a_ssq", "a_sqrt", "a_rope", "a_qkT", "a_qkS", "a_sc", "a_max", "a_exp",
             "a_rec", "a_norm", "a_pT", "a_pTs", "a_pv", "a_ohi", "a_o"))
        s_neg = sem("s_neg")
        (s_pre, s_in, s_zin, s_loc, s_Tin, s_cin, s_tap, s_silu, s_zs, s_Tb, s_cb, s_tok, s_dc, s_D, s_E, s_xw,
         s_H, s_S, s_M, s_h0, s_ht, s_h1, s_yo, s_yd, s_y1, s_y2, s_y3, s_yz, s_sqa, s_sq, s_rec, s_y,
         s_yst) = map(sem, (
             "s_pre", "s_in", "s_zin", "s_loc", "s_Tin", "s_cin", "s_tap", "s_silu", "s_zs", "s_Tb", "s_cb",
             "s_tok", "s_dc", "s_D", "s_E", "s_xw", "s_H", "s_S", "s_M", "s_h0", "s_ht", "s_h1", "s_yo", "s_yd",
             "s_y1", "s_y2", "s_y3", "s_yz", "s_sqa", "s_sq", "s_rec", "s_y", "s_yst"))
        y_in, xres_in, g_in, g_sig, g_tmp, g_ev = map(sem, ("y_in", "xres_in", "g_in", "g_sig", "g_tmp", "g_ev"))
        dg_ready, dg_T, gt_ready, o_tmp, o_ev = map(sem, ("dg_ready", "dg_T", "gt_ready", "o_tmp", "o_ev"))
        xm_out, f_T, f_hi, f_lo = map(sem, ("xm_out", "f_T", "f_hi", "f_lo"))
        f2_in, f2_tmp, f2_ev, f2_out = map(sem, ("f2_in", "f2_tmp", "f2_ev", "f2_out"))

        block = outer.enter_context(nc.Block())

        def rows2(view, c0, n):
            return view.rearrange("(t p) n -> p t n", p=P)[:, :, bass.ds(c0, n)]

        def col(table, p):
            return [row[p] for row in table]

        def last_chunk(ph, b):
            return 4 * (b // 2) + 3 if len(ph.banks) > len(ph.tiles) else ph.chunks - 1

        def wait_bank(eng, ph, i, b):
            if b % len(ph.tiles) == len(ph.tiles) - 1:
                eng.wait_ge(pe_used, lin(col(ph.index, last_chunk(ph, b)), i) + 1)
            else:
                before = b // len(ph.tiles) * (len(ph.tiles) - 1) + b % len(ph.tiles)
                eng.wait_ge(bank_done, lin(ph.done0, i) + before + 1)

        def wait_split_slot(eng, ph, i, p):
            prev = col(ph.spl_prev, p)
            if isinstance(i, int):
                if prev[i] is not None:
                    eng.wait_ge(pe_used, prev[i] + 1)
            else:
                eng.wait_ge(pe_used, lin(prev, i) + 1)

        G_LAT, G_CTX, G_Y, G_M, G_H2 = 0, 8, 16, 24, 32

        def transpose_groups(pe, first, rows_of):
            for m in range(8):
                g = first + m
                if g >= 2:
                    pe.wait_ge(tp_tmp, g - 1)
                for k in range(2):
                    for t in range(2):
                        last = nc.tensor.transpose(PS[:, 4 + g % 2, k * T + t * P:k * T + (t + 1) * P],
                                                   rows_of(t, 2 * m + k), ident[:, :])
                last.then_inc(tp_done, 1)

        def high_groups(act, first, hi, k0):
            for m in range(8):
                g = first + m
                act.wait_ge(tp_tmp, g + 1)
                nc.scalar.activation(hi[:, k0 + 2 * m:k0 + 2 * m + 2, :], tmp[:, g % 2, :, :],
                                     ACT.Copy).then_inc(tp_hi, 1)

        def low_groups(dve, first, hi, lo, k0, scale, shift):
            def copy_out(m):
                g = first + m
                dve.wait_ge(tp_done, g + 1)
                if g >= 2:
                    dve.wait_ge(tp_hi, g - 1)
                    dve.wait_ge(tp_lo, g - 1)
                for k in range(2):
                    src = PS[:, 4 + g % 2, k * T:(k + 1) * T]
                    dst = tmp[:, g % 2, k, :]
                    if shift is not None:
                        ins = nc.vector.tensor_scalar(dst, src, scale(2 * m + k), shift(2 * m + k), ALU.mult, ALU.add)
                    elif scale is not None:
                        ins = nc.vector.tensor_scalar(dst, src, scale(2 * m + k), None, ALU.mult)
                    else:
                        ins = nc.vector.tensor_copy(dst, src)
                ins.then_inc(tp_tmp, 1)

            def low(m):
                g = first + m
                dve.wait_ge(tp_hi, g + 1)
                dve.wait_ge(tp_tmp, g + 1)
                ks = slice(k0 + 2 * m, k0 + 2 * m + 2)
                nc.vector.tensor_tensor(lo[:, ks, :], tmp[:, g % 2, :, :], hi[:, ks, :].bitcast(F32),
                                        ALU.subtract).then_inc(tp_lo, 1)

            copy_out(0)
            for m in range(8):
                if m < 7:
                    copy_out(m + 1)
                low(m)

        @block.sync
        def _(sp):
            def load(ph, i, p):
                prev = col(ph.raw_prev, p)
                s = p % RAW
                user = prev[i if isinstance(i, int) else 1]
                if user is not None:
                    idx = user[1] if isinstance(i, int) else lin([u[1] if u else None for u in prev], i)
                    sp.wait_ge(mod_used if user[0] == "mod" else lo_ready, idx + 1)
                if ph is p_dt:
                    dst = raw[:, s, :, :].rearrange("p k n -> p (k n)")[:, 0:KT * 64].rearrange(
                        "p (k n) -> p k n", n=64)
                    sp.dma_start(dst, w_dt).then_inc(raw_loaded[s], 16)
                else:
                    sp.dma_start(raw[:, s, :, :], source(ph, i, p)).then_inc(raw_loaded[s], 16)

            for ph in phases:
                each_block(sp, ph.n, lambda i: [load(ph, i, p) for p in range(ph.chunks)])

        @block.gpsimd
        def _(pool):
            pool.dma_start(x_tok[:, 0:2, :], x_in).then_inc(x_loaded, 16)
            pool.dma_start(x_tok[:, 2:4, :], ctx_in).then_inc(x_loaded, 16)

            def all_stored(ph):
                for b in range(4):
                    pool.wait_ge(stored[b], ph.staged_end[b])

            all_stored(p_c)
            pool.wait_ge(bank_free, p_c.banks_end)
            pool.wait_ge(n_mul, 4)
            pool.wait_ge(tp_done, G_Y)
            pool.dma_start(rope[:, :, 0, :], a["rope_cos"].rearrange("(t p) n -> p t n", p=P)).then_inc(r_in, 16)
            pool.dma_start(rope[:, :, 1, :], a["rope_sin"].rearrange("(t p) n -> p t n", p=P)).then_inc(r_in, 16)
            for h in range(REP):
                pool.dma_start(gain5[:, h, :], a["q_norm"][0:1, :].to_broadcast([P, AD])).then_inc(r_in, 16)
            pool.dma_start(gain5[:, 4, :], a["k_norm"][0:1, :].to_broadcast([P, AD])).then_inc(r_in, 16)

            def attention_loads(i):
                if not (isinstance(i, int) and i == 0):
                    pool.wait_ge(a_rope, i * 1)
                    pool.wait_ge(a_qkT, i * 1)
                for t in range(2):
                    pool.dma_start(qk[:, 5 * t:5 * t + 4, :], proj_lat[t * P:(t + 1) * P, bass.ds(i * 512 + CQ, 512)]
                                   .rearrange("p (h d) -> p h d", d=AD)).then_inc(a_in, 16)
                    pool.dma_start(qk[:, 5 * t + 4, :], proj_lat[t * P:(t + 1) * P, bass.ds(i * AD + CK, AD)]
                                   ).then_inc(a_in, 16)
                pool.dma_start(qk[:, 10:12, :], rows2(proj_ctx, i * AD + CK, AD)).then_inc(a_in, 16)
                if not (isinstance(i, int) and i == 0):
                    pool.wait_ge(a_pv, i * REP)
                pool.dma_start(vv[:, 0:2, :], rows2(proj_ctx, i * AD + CV, AD)).then_inc(a_vin, 16)
                pool.dma_start(vv[:, 2:4, :], rows2(proj_lat, i * AD + CV, AD)).then_inc(a_vin, 16)

            each_block(pool, KVH, attention_loads)

            all_stored(p_z)
            pool.wait_ge(a_o, AH)
            nc.gpsimd.memset(cin[:, :, 0:2], 0.0)
            nc.gpsimd.memset(cin[:, :, T + 2:T + 4], 0.0).then_inc(s_pre, 1)

            def ssd_loads(g):
                if not (isinstance(g, int) and g == 0):
                    pool.wait_ge(s_Tin, g * 1)
                for view, u, c0, n, o in ((proj_lat, u_lat, g * 256 + CX, 256, 0), (proj_lat, u_lat, g * NST + CB, NST, 256),
                                          (proj_lat, u_lat, g * NST + CC, NST, 384), (proj_ctx, u_ctx, g * 256 + CX, 256, 0),
                                          (proj_ctx, u_ctx, g * NST + CB, NST, 256)):
                    pool.dma_start(u[:, :, o:o + n], rows2(view, c0, n)).then_inc(s_in, 16)
                if not (isinstance(g, int) and g == 0):
                    pool.wait_ge(s_yz, g * 1)
                pool.dma_start(zt[:, :, :], rows2(proj_lat, g * 256 + CZ, 256)).then_inc(s_zin, 16)

            each_block(pool, GROUPS, ssd_loads)

            all_stored(p_g)
            pool.wait_ge(s_yst, 16 * GROUPS)
            pool.dma_start(wide[:, :, :], y_dram.rearrange("(t p) n -> p t n", p=P)).then_inc(y_in, 16)
            pool.dma_start(xres[:, :, :], x_in).then_inc(xres_in, 16)

            def gate_loads(i):
                if not (isinstance(i, int) and i == 0):
                    pool.wait_ge(g_ev, i * 1)
                pool.dma_start(gates[:, 0, :, :], rows2(proj_lat, i * NB + CG + D, NB)).then_inc(g_in, 16)
                pool.dma_start(gates[:, 1, :, :], rows2(proj_lat, i * NB + CG, NB)).then_inc(g_in, 16)

            each_block(pool, 4, gate_loads)
            pool.wait_ge(gt_ready, 8)
            pool.dma_start(gate2_dram, wide[0:1, 0, :]).then_inc(xm_out, 16)
            pool.wait_ge(xm_out, 16)
            pool.wait_ge(o_ev, 4)
            pool.dma_start(xmid_dram.rearrange("(t p) n -> p t n", p=P), xres[:, :, :]).then_inc(xm_out, 16)
            pool.wait_ge(xm_out, 32)
            pool.wait_ge(f_lo, DFF // NB)

            def out_step(i):
                if not (isinstance(i, int) and i == 0):
                    pool.wait_ge(f2_ev, i * 1)
                pool.dma_start(stage[:, 0:2, :], rows2(xmid_dram, i * NB, NB)).then_inc(f2_in, 16)
                pool.dma_start(tmp[:, 0, :, :].rearrange("p a b -> p (a b)"),
                               gate2_dram[:, bass.ts(i, NB)].to_broadcast([P, NB])).then_inc(f2_in, 16)

            each_block(pool, 4, out_step)

        @block.tensor
        def _(pe):
            def chunk(ph, i, p, acts, banks, kt0, first, final):
                pe.wait_ge(hi_ready, lin(col(ph.index, p), i) + 1)
                pe.wait_ge(lo_ready, lin(col(ph.index, p), i) + 1)
                s = p % SPL
                n, ks = (64, KT) if ph is p_dt else (NB, CK_T)
                hi_w = w_hi[:, s, :, :].rearrange("p k n -> p (k n)")[:, 0:ks * n].rearrange("p (k n) -> p k n", n=n)
                lo_w = w_lo[:, s, :, :].rearrange("p k n -> p (k n)")[:, 0:ks * n].rearrange("p (k n) -> p k n", n=n)
                for t, b in enumerate(banks):
                    if first:
                        prior = ph.banks.index(b) + 1
                        if isinstance(i, int) and i == 0:
                            if t == 0:
                                pe.wait_ge(bank_free, ph.bank0[0])
                        else:
                            pe.wait_ge(bank_free, lin(ph.bank0, i) - len(ph.banks) + prior)
                    dst = PS[:, b, 0:n]
                    toks = slice((t % 2) * P, (t % 2 + 1) * P)
                    for k in range(ks):
                        kt = kt0 + (16 if t >= 2 else 0) + k
                        x_hi, x_lo = acts[0][:, kt, toks], acts[1][:, kt, toks]
                        begin, end = first and k == 0, final and k == ks - 1
                        nc.tensor.matmul(dst, x_hi, hi_w[:, k, :], start=begin, stop=False)
                        nc.tensor.matmul(dst, x_hi, lo_w[:, k, :], start=False, stop=False)
                        last = nc.tensor.matmul(dst, x_lo, hi_w[:, k, :], start=False, stop=end)
                    if final and t < len(banks) - 1:
                        last.then_inc(bank_done, 1)
                last.then_inc(pe_used, 1)

            act1, act2 = (act1_hi, act1_lo), (act2_hi, act2_lo)

            def plain(ph, i, p):
                chunk(ph, i, p, act1, ph.banks, p * CK_T, p == 0, p == ph.chunks - 1)

            pe.wait_ge(setup_in, SETUP * 16)
            pe.wait_ge(c_silu, 1)
            o = 0
            for r, n in enumerate((96, 80, 128, 32)):
                nc.tensor.transpose(PS[:, 4, o:o + n], rows[0:n, r, :], ident[0:n, 0:n])
                o += n
            nc.tensor.transpose(PS[:, 4, o:o + 32], c_rows[:, :], ident[0:32, 0:32]).then_inc(vec_T, 1)

            pe.wait_ge(cols_ready, 5)
            cond = c_col[:, :].rearrange("p (w k) -> p k w", w=2)

            def mod_block(i):
                for p in range(4):
                    pe.wait_ge(raw_loaded[p], lin(col(p_mod.loaded, p), i))
                    for j in range(4):
                        for k in range(CK_T):
                            last = nc.tensor.matmul(PS[:, 6, bass.ds(i * 8 + 2 * j, 2)], raw[:, p, k, j * P:(j + 1) * P],
                                                    cond[:, p * CK_T + k, :], start=(p == 0 and j == 0 and k == 0),
                                                    stop=(p == 3 and k == 3), skip_group_check=True)
                    last.then_inc(mod_used, 1)

            each_block(pe, p_mod.n, mod_block)

            for t in range(4):
                if t % 2 == 0:
                    pe.wait_ge(n_mul, t + 2)
                    transpose_groups(pe, G_LAT if t == 0 else G_CTX,
                                     lambda tt, k: x_tok[:, t + tt, k * P:(k + 1) * P])
            pe.wait_ge(tp_lo, G_Y)

            for ph in (p_kv, p_xb, p_dt):
                each_block(pe, ph.n, lambda i: [plain(ph, i, p) for p in range(ph.chunks)])

            pe.wait_ge(d_dve, D_A)
            pe.wait_ge(consts, 1)
            for ch in range(4):
                for d in range(2):
                    nc.tensor.matmul(PS[:, 7, ch * 64 + d * 32:ch * 64 + d * 32 + 32], tri[:, d, :],
                                     av[:, ch, d * 32:d * 32 + 32], start=True, stop=True)
            nc.tensor.matmul(PS[:, 7, 256:512], ones[:, :], av[:, :, :].rearrange("p a b -> p (a b)"),
                             start=True, stop=True).then_inc(d_pe, 1)

            for ph in (p_q, p_c):
                each_block(pe, ph.n, lambda i: [plain(ph, i, p) for p in range(ph.chunks)])

            def scores(i, u):
                h, t = u // 2, u % 2
                if not (isinstance(i, int) and i == 0 and u < 2):
                    pe.wait_ge(a_exp, i * 8 + (u - 1))
                nc.tensor.matmul(PS[:, 2 + u % 2, :], qT[:, h, t * P:(t + 1) * P], kT[:, :],
                                 start=True, stop=True).then_inc(a_sc, 1)

            def turn_probs(i, u):
                pe.wait_ge(a_norm, i * 8 + (u + 1))
                if not (isinstance(i, int) and i == 0 and u < 2):
                    pe.wait_ge(a_pTs, i * 8 + (u - 1))
                for k in range(4):
                    last = nc.tensor.transpose(PS[:, 4 + u % 2, k * P:(k + 1) * P], probs[:, u % 2, k * P:(k + 1) * P],
                                               ident[:, :])
                last.then_inc(a_pT, 1)

            def values(i, h):
                pe.wait_ge(a_pTs, i * 8 + (2 * h + 2))
                pe.wait_ge(a_vin, i * 32 + 32)
                if not (isinstance(i, int) and i == 0 and h < 2):
                    pe.wait_ge(a_o, i * REP + (h - 1))
                for k in range(4):
                    last = nc.tensor.matmul(PS[:, 6 + h % 2, 0:T], vv[:, k, :], pT[:, h % 2, k, :],
                                            start=(k == 0), stop=(k == 3))
                last.then_inc(a_pv, 1)

            def attention_start(i):
                pe.wait_ge(a_rope, i + 1)
                if not (isinstance(i, int) and i == 0):
                    pe.wait_ge(a_pTs, i * 8)
                    pe.wait_ge(a_o, i * REP)
                for h in range(REP):
                    for t in range(2):
                        nc.tensor.transpose(PS[:, 4 + h // 2, (h % 2) * T + t * P:(h % 2) * T + (t + 1) * P],
                                            qk_r[:, 5 * t + h, :], ident[:, :])
                for t in range(2):
                    nc.tensor.transpose(PS[:, 6, t * P:(t + 1) * P], qk[:, 10 + t, :], ident[:, :])
                    last = nc.tensor.transpose(PS[:, 6, (2 + t) * P:(3 + t) * P], qk_r[:, 5 * t + 4, :], ident[:, :])
                last.then_inc(a_qkT, 1)
                pe.wait_ge(a_qkS, i + 1)

            def attention_steps(i, lo, hi):
                for s in range(lo, hi):
                    if s < 8:
                        scores(i, s)
                    if 1 <= s <= 8:
                        turn_probs(i, s - 1)
                    if s >= 3 and s % 2 == 1:
                        values(i, (s - 3) // 2)

            pe.wait_ge(d_act, 6)
            pe.wait_ge(d_dve, D_END)

            def z_step(i):
                plain(p_z, i, 0)
                attention_start(i)
                attention_steps(i, 0, 2)
                plain(p_z, i, 1)
                attention_steps(i, 2, 5)
                plain(p_z, i, 2)
                attention_steps(i, 5, 8)
                plain(p_z, i, 3)
                attention_steps(i, 8, 10)

            each_block(pe, p_z.n, z_step)

            def conv_in(g):
                pe.wait_ge(s_in, g * 80 + 80)
                if isinstance(g, int) and g == 0:
                    pe.wait_ge(a_o, AH)
                    pe.wait_ge(a_pTs, 8 * KVH)
                else:
                    pe.wait_ge(s_yz, g * 1)
                for m in range(7):
                    for t in range(2):
                        src = u_lat[:, t, m * P:(m + 1) * P] if m < 4 else u_ctx[:, t, (m - 4) * P:(m - 3) * P]
                        last = nc.tensor.transpose(PS[:, 2 + m // 2, (m % 2) * T + t * P:(m % 2) * T + (t + 1) * P],
                                                   src, ident[:, :])
                last.then_inc(s_Tin, 1)

            def back_to_rows(g):
                pe.wait_ge(s_silu, g + 1)
                for ch in range(4):
                    t = ch % 2
                    for j in range(3):
                        tile = j if ch >= 2 else 4 + j
                        last = nc.tensor.transpose(PS[:, 2 + ch, j * P:(j + 1) * P], cv[:, tile, t * P:(t + 1) * P],
                                                   ident[:, :])
                last.then_inc(s_Tb, 1)
                for c in range(2):
                    last = nc.tensor.matmul(PS[:, 6, c * P:(c + 1) * P], cv[:, 2, c * P:(c + 1) * P],
                                            cv[:, 3, c * P:(c + 1) * P], start=True, stop=True)
                last.then_inc(s_cb, 1)

            def decays(g):
                pe.wait_ge(s_tok, g + 1)
                pe.wait_ge(s_loc, g + 1)
                pe.wait_ge(s_neg, 1)
                for c in range(2):
                    for d in range(2):
                        bank = PS[:, 2 + 2 * c + d, :]
                        nc.tensor.matmul(bank, ident[:, :], negm[:, d, :].unsqueeze(1).to_broadcast([P, HPG, P]),
                                         start=True, stop=False, skip_group_check=True)
                        for h in range(HPG):
                            last = nc.tensor.matmul(bank[:, h * P:(h + 1) * P],
                                                    a_loc[:, c, d, h:h + 1].to_broadcast([P, P]), tri[:, d, :],
                                                    start=False, stop=True, skip_group_check=True)
                last.then_inc(s_dc, 1)

            def states(g):
                pe.wait_ge(s_xw, g + 1)
                for d, xd in ((0, xdf), (1, xdb)):
                    for ch in range(2):
                        last = nc.tensor.matmul(PS[:, 7, d * 256:(d + 1) * 256], tokb[:, ch, 256:384], xd[:, ch, :],
                                                start=(ch == 0), stop=(ch == 1))
                last.then_inc(s_H, 1)
                pe.wait_ge(s_D, g * 4 + 4)
                nc.tensor.matmul(PS[:, 2, 0:256], tokb[:, 2, 256:384], xdf[:, 2, :], start=True, stop=True)
                nc.tensor.matmul(PS[:, 2, 256:512], tokb[:, 3, 256:384], xdb[:, 2, :],
                                 start=True, stop=True).then_inc(s_S, 1)

            def outputs(g):
                pe.wait_ge(s_h0, g + 1)
                pe.wait_ge(s_h1, g + 1)
                for c in range(2):
                    last = nc.tensor.matmul(PS[:, 3 + c, :], cv[:, 3, c * P:(c + 1) * P],
                                            hst[:, c, :, :].rearrange("p d n -> p (d n)"), start=True, stop=True)
                last.then_inc(s_yo, 1)
                pe.wait_ge(s_M, g + 1)
                for c in range(2):
                    for h in range(HPG):
                        for d in range(2):
                            last = nc.tensor.matmul(PS[:, 5, c * 256 + h * HD:c * 256 + (h + 1) * HD],
                                                    dec[:, 2 * c + d, h, :], xdt[:, d, c, h * HD:(h + 1) * HD],
                                                    start=(d == 0), stop=(d == 1))
                last.then_inc(s_yd, 1)

            def g_step(i):
                conv_in(i)
                plain(p_g, i, 0)
                plain(p_g, i, 1)
                back_to_rows(i)
                decays(i)
                plain(p_g, i, 2)
                states(i)
                plain(p_g, i, 3)
                outputs(i)

            each_block(pe, p_g.n, g_step)

            pe.wait_ge(s_yz, GROUPS)
            pe.wait_ge(y_in, 16)
            transpose_groups(pe, G_Y, lambda t, k: wide[:, t, k * P:(k + 1) * P])
            pe.wait_ge(tp_lo, G_M)

            def br_block(i):
                for p in range(8):
                    chunk(p_br, i, p, act1, [0, 1] if p < 4 else [2, 3], (16 if p < 4 else 0) + (p % 4) * CK_T,
                          p % 4 == 0, p % 4 == 3)

            each_block(pe, p_br.n, br_block)
            for m in range(8):
                if m == 4:
                    pe.wait_ge(g_ev, 4)
                    transpose_groups(pe, G_M, lambda t, k: wide[:, t, k * P:(k + 1) * P])
                pe.wait_ge(dg_ready, m + 1)
                if m >= 1:
                    pe.wait_ge(gt_ready, m)
                nc.tensor.matmul(PS[:, 7, :], ones[:, :], diag[:, :, :].rearrange("p a b -> p (a b)"),
                                 start=True, stop=True).then_inc(dg_T, 1)
            pe.wait_ge(tp_lo, G_H2)
            each_block(pe, p_o.n, lambda i: [plain(p_o, i, p) for p in range(4)])
            pe.wait_ge(n_mul, 6)
            transpose_groups(pe, G_H2, lambda t, k: wide[:, t, k * P:(k + 1) * P])
            pe.wait_ge(tp_lo, G_H2 + 8)

            def f1_chunk(i, p):
                chunk(p_f1, i, p, act2, [0, 1] if p < 4 else [2, 3], H2 + (p % 4) * CK_T, p % 4 == 0, p % 4 == 3)

            def turn_hidden(i):
                pe.wait_ge(bank_free, lin(p_f1.bank0, i) + 4)
                if not (isinstance(i, int) and i == 0):
                    pe.wait_ge(f_lo, i * 1)
                for k in range(4):
                    for t in range(2):
                        last = nc.tensor.transpose(PS[:, 4 + k // 2, (k % 2) * T + t * P:(k % 2) * T + (t + 1) * P],
                                                   stage[:, t, k * P:(k + 1) * P], ident[:, :])
                last.then_inc(f_T, 1)

            def f1_block(i):
                for p in range(8):
                    f1_chunk(i, p)
                    if p == 1 and not (isinstance(i, int) and i == 0):
                        turn_hidden(i - 1)

            each_block(pe, p_f1.n, f1_block)
            turn_hidden(p_f1.n - 1)
            pe.wait_ge(f_lo, p_f1.n)
            each_block(pe, p_f2.n, lambda i: [chunk(p_f2, i, p, act2, LAT, p * CK_T, p == 0, p == p_f2.chunks - 1)
                                              for p in range(p_f2.chunks)])

        @block.scalar
        def _(act):
            small = [(ident[:, :], a["c_ident"]), (tri[:, 0, :], a["c_tri_f"]), (tri[:, 1, :], a["c_tri_b"]),
                     (rows[0:96, 0, :], a["b_mod"][0].rearrange("(r c) -> r c", c=P)),
                     (rows[0:16, 1, :], a["norm1"][0].rearrange("(r c) -> r c", c=P)),
                     (rows[16:32, 1, :], a["norm2"][0].rearrange("(r c) -> r c", c=P)),
                     (rows[32:48, 1, :], a["ssm_norm"][0].rearrange("(r c) -> r c", c=P)),
                     (rows[48:80, 1, :], a["conv_b"][0].rearrange("(r c) -> r c", c=P)),
                     (rows[:, 2, :], a["conv_w"][0].rearrange("j (r c) -> (j r) c", c=P)[0:P, :]),
                     (rows[0:32, 3, :], a["conv_w"][0].rearrange("j (r c) -> (j r) c", c=P)[P:P + 32, :]),
                     (c_rows[0:16, :], a["c"][0].rearrange("(r c) -> r c", c=P)),
                     (c_rows[16:32, :], a["c_ctx"].rearrange("(r c) -> r c", c=P)),
                     (dskip[:, :], a["d_skip"][0:1, :].to_broadcast([P, HEADS])),
                     (dtb[:, :], a["dt_bias"].rearrange("a d h -> a (d h)").to_broadcast([P, 64])),
                     (aneg[:, :], a["a_log"].rearrange("a d h -> a (d h)").to_broadcast([P, 64]))]
            assert len(small) == SETUP
            for dst, src in small:
                act.dma_start(dst, src).then_inc(setup_in, 16)
            act.wait_ge(setup_in, 16 * SETUP)
            nc.scalar.activation(c_rows[:, :], c_rows[:, :], ACT.Silu).then_inc(c_silu, 1)
            nc.scalar.activation(aneg[:, :], aneg[:, :], ACT.Exp).then_inc(c_silu, 1)

            act.wait_ge(x_loaded, 32)
            for t in range(4):
                if t > 0:
                    act.wait_ge(n_sq, t)
                nc.scalar.activation(junk, x_tok[:, t, :], ACT.Square, accum_out=stat[:, t:t + 1]).then_inc(n_sq, 1)
            act.wait_ge(n_sq, 4)
            act.wait_ge(consts, 2)
            nc.scalar.activation(stat[:, 4:8], stat[:, 0:4], ACT.Sqrt, scale=1.0 / D,
                                 bias=stat[:, 15:16]).then_inc(n_sqrt, 1)
            high_groups(act, G_LAT, act1_hi, 0)
            high_groups(act, G_CTX, act1_hi, 16)

            def high(ph, i, p):
                act.wait_ge(raw_loaded[p % RAW], lin(col(ph.loaded, p), i))
                wait_split_slot(act, ph, i, p)
                dst, src = w_hi[:, p % SPL, :, :], raw[:, p % RAW, :, :]
                if ph is p_dt:
                    dst, src = [v.rearrange("p k n -> p (k n)")[:, 0:KT * 64] for v in (dst, src)]
                nc.scalar.activation(dst, src, ACT.Copy).then_inc(hi_ready, 1)

            def stage_out(ph, i):
                for b, bank in enumerate(ph.banks):
                    wait_bank(act, ph, i, b)
                    if not isinstance(i, int) or ph.stage0[i][b]:
                        act.wait_ge(stored[b], lin([s[b] for s in ph.stage0], i))
                    nc.scalar.activation(stage[:, b, :], PS[:, bank, :], ACT.Copy).then_inc(bank_free, 1)
                for b in range(len(ph.banks)):
                    act.wait_ge(bank_free, lin(ph.bank0, i) + b + 1)
                    dst = (proj_lat if b < 2 else proj_ctx)[(b % 2) * P:(b % 2 + 1) * P,
                                                            bass.ds(i * NB + PROJ_COL[ph.name], NB)]
                    act.dma_start(dst, stage[:, b, :]).then_inc(stored[b], 16)

            pending = [lambda: None]

            def stream(ph, evac, after=lambda i, p: None):
                def body(i):
                    for p in range(ph.chunks):
                        high(ph, i, p)
                        if p == 0:
                            if isinstance(i, int) and i == 0:
                                pending[0]()
                            else:
                                evac(i - 1)
                        after(i, p)
                each_block(act, ph.n, body)
                pending[0] = lambda: evac(ph.n - 1)

            stream(p_kv, lambda i: stage_out(p_kv, i))
            stream(p_xb, lambda i: stage_out(p_xb, i))
            stream(p_dt, lambda i: None)
            act.wait_ge(bank_free, p_dt.banks_end)
            nc.scalar.activation(av[:, :, :], dt[:, :, :], ACT.Abs).then_inc(d_act, 1)
            act.wait_ge(d_act, 1)
            nc.scalar.activation(av[:, :, :], av[:, :, :], ACT.Exp, scale=-1.0).then_inc(d_act, 1)
            act.wait_ge(d_dve, 1)
            nc.scalar.activation(etot[:, :, :], acum[:, :, :], ACT.Ln).then_inc(d_act, 1)
            act.wait_ge(d_dve, D_A + 2)
            nc.scalar.activation(etot[:, :, :].rearrange("p a b -> p (a b)"), PS[:, 7, 256:512],
                                 ACT.Exp).then_inc(d_act, 1)
            nc.scalar.activation(eacum[:, :, :].rearrange("p a b -> p (a b)"), PS[:, 7, 0:256],
                                 ACT.Exp).then_inc(d_act, 1)
            nc.scalar.activation(wdec[:, :, :], wdec[:, :, :], ACT.Exp).then_inc(d_act, 1)

            stream(p_q, lambda i: stage_out(p_q, i))
            stream(p_c, lambda i: stage_out(p_c, i))

            def attention_start(i):
                act.wait_ge(a_ssq, i + 1)
                nc.scalar.activation(ast[:, 12:24], ast[:, 0:12], ACT.Sqrt, scale=1.0 / AD,
                                     bias=stat[:, 15:16]).then_inc(a_sqrt, 1)
                act.wait_ge(a_qkT, i + 1)
                if not (isinstance(i, int) and i == 0):
                    act.wait_ge(a_sc, i * 8)
                nc.scalar.activation(qT[:, :, :].rearrange("p (b h) t -> p b (h t)", b=2), PS[:, 4:6, :], ACT.Copy)
                nc.scalar.activation(kT[:, :], PS[:, 6, :], ACT.Copy).then_inc(a_qkS, 1)

            def attention_steps(i, lo, hi):
                for s in range(lo, hi):
                    if s < 8:
                        act.wait_ge(a_max, i * 8 + (s + 1))
                        if not (isinstance(i, int) and i == 0 and s < 2):
                            act.wait_ge(a_pT, i * 8 + (s - 1))
                        nc.scalar.activation(probs[:, s % 2, :], PS[:, 2 + s % 2, :], ACT.Exp,
                                             bias=ast[:, 36 + s % 2:37 + s % 2],
                                             accum_out=ast[:, 40 + s % 2:41 + s % 2]).then_inc(a_exp, 1)
                    if 2 <= s <= 9:
                        u = s - 2
                        h, t = u // 2, u % 2
                        act.wait_ge(a_pT, i * 8 + (u + 1))
                        if not (isinstance(i, int) and i == 0 and h < 2):
                            act.wait_ge(a_pv, i * REP + (h - 1))
                        nc.scalar.activation(pT[:, h % 2, :, t * P:(t + 1) * P],
                                             PS[:, 4 + u % 2, :].rearrange("p (k q) -> p k q", k=4),
                                             ACT.Copy).then_inc(a_pTs, 1)
                    if s >= 4 and s % 2 == 0:
                        h = (s - 4) // 2
                        act.wait_ge(a_pv, i * REP + (h + 1))
                        nc.scalar.activation(act1_hi[:, bass.ds(i * REP + (16 + h), 1), :], PS[:, 6 + h % 2, 0:T],
                                             ACT.Copy).then_inc(a_ohi, 1)

            def z_after(i, p):
                if p == 0:
                    attention_start(i)
                attention_steps(i, *((0, 2), (2, 5), (5, 8), (8, 11))[p])

            stream(p_z, lambda i: stage_out(p_z, i), z_after)

            def store_y(g):
                act.wait_ge(s_y, g + 1)
                act.dma_start(rows2(y_dram, g * 256, 256), yb[:, :, :]).then_inc(s_yst, 16)

            def g_after(g, p):
                if p == 1 and not (isinstance(g, int) and g == 0):
                    store_y(g - 1)
                if p == 0:
                    act.wait_ge(s_Tin, g + 1)
                    if isinstance(g, int) and g == 0:
                        act.wait_ge(s_pre, 1)
                    for q in range(4):
                        m = 2 if q < 3 else 1
                        last = nc.scalar.activation(cin[:, 2 * q:2 * q + m, 2:T + 2],
                                                    PS[:, 2 + q, 0:m * T].rearrange("p (m t) -> p m t", t=T), ACT.Copy)
                    last.then_inc(s_cin, 1)
                if p == 1:
                    act.wait_ge(s_tap, g * TAPS + TAPS)
                    for m in range(7):
                        tile = g * 2 + (48 + m % 4) if m % 4 < 2 else g + (48 + 16 if m % 4 == 2 else 48 + 24)
                        last = nc.scalar.activation(cv[:, m, :], cv[:, m, :], ACT.Silu, bias=vec_col[:, bass.ds(tile, 1)])
                    last.then_inc(s_silu, 1)
                    act.wait_ge(s_zin, g * 16 + 16)
                    nc.scalar.activation(zt[:, :, :], zt[:, :, :], ACT.Silu).then_inc(s_zs, 1)
                    act.wait_ge(s_Tb, g + 1)
                    for ch in range(4):
                        last = nc.scalar.activation(tokb[:, ch, :], PS[:, 2 + ch, 0:384], ACT.Copy)
                    last.then_inc(s_tok, 1)
                if p == 2:
                    act.wait_ge(s_D, g * 4 + 4)
                    nc.scalar.activation(dec[:, :, :, :], dec[:, :, :, :], ACT.Exp).then_inc(s_E, 1)
                    act.wait_ge(s_H, g + 1)
                    nc.scalar.activation(hst[:, 0, 0, :], PS[:, 7, 0:256], ACT.Copy)
                    nc.scalar.activation(hst[:, 1, 1, :], PS[:, 7, 256:512], ACT.Copy).then_inc(s_h0, 1)
                if p == 3:
                    act.wait_ge(s_yz, g + 1)
                    for c in range(2):
                        last = nc.scalar.activation(yt[:, c, 0:256], yb[:, c, :], ACT.Square,
                                                    accum_out=sst[:, c:c + 1])
                    last.then_inc(s_sqa, 1)
                    act.wait_ge(s_sqa, g + 1)
                    nc.scalar.activation(sst[:, 2:4], sst[:, 0:2], ACT.Sqrt, scale=1.0 / 256,
                                         bias=stat[:, 15:16]).then_inc(s_sq, 1)

            stream(p_g, lambda i: stage_out(p_g, i), g_after)
            store_y(GROUPS - 1)
            pending[0]()
            high_groups(act, G_Y, act1_hi, 0)

            def br_after(i, p):
                if p == 4:
                    act.wait_ge(g_in, i * 32 + 32)
                    nc.scalar.activation(gates[:, :, :, :], gates[:, :, :, :], ACT.Sigmoid).then_inc(g_sig, 1)

            pending[0] = lambda: None
            stream(p_br, lambda i: None, br_after)
            for m in range(8):
                act.wait_ge(dg_T, m + 1)
                if m == 4:
                    act.wait_ge(tp_done, G_H2)
                dst = gt1[:, m * NB:(m + 1) * NB] if m < 4 else wide[:, 0, (m - 4) * NB:(m - 3) * NB]
                if m < 4:
                    nc.scalar.activation(dst, PS[:, 7, :], ACT.Copy).then_inc(gt_ready, 1)
                else:
                    nc.scalar.activation(dst, PS[:, 7, :], ACT.Copy).then_inc(gt_ready, 1)
                if m == 3:
                    high_groups(act, G_M, act1_hi, 0)
            stream(p_o, lambda i: None)
            act.wait_ge(o_ev, 4)
            for t in range(2):
                if t > 0:
                    act.wait_ge(n_sq, 4 + t)
                nc.scalar.activation(junk, xres[:, t, :], ACT.Square, accum_out=stat[:, 8 + t:9 + t]).then_inc(n_sq, 1)
            act.wait_ge(n_sq, 6)
            nc.scalar.activation(stat[:, 10:12], stat[:, 8:10], ACT.Sqrt, scale=1.0 / D,
                                 bias=stat[:, 15:16]).then_inc(n_sqrt, 1)
            act.wait_ge(pe_used, p_o.index[-1][-1] + 1)
            high_groups(act, G_H2, act2_hi, H2)

            def gate_out(i):
                for t in range(2):
                    wait_bank(act, p_f1, i, t)
                    if not (isinstance(i, int) and i == 0):
                        act.wait_ge(f_T, i * 1)
                    nc.scalar.activation(stage[:, t, :], PS[:, t, :], ACT.Silu).then_inc(bank_free, 1)

            def hidden_high(i):
                act.wait_ge(f_T, i + 1)
                nc.scalar.activation(act2_hi[:, bass.ds(i * 4, 4), :].rearrange("p (b k) t -> p b (k t)", b=2),
                                     PS[:, 4:6, :], ACT.Copy).then_inc(f_hi, 1)

            def f1_after(i, p):
                if p == 2 and not (isinstance(i, int) and i == 0):
                    hidden_high(i - 1)

            stream(p_f1, gate_out, f1_after)
            pending[0] = lambda: (gate_out(p_f1.n - 1), hidden_high(p_f1.n - 1))
            def store_out(i):
                act.wait_ge(f2_ev, i + 1)
                act.dma_start(rows2(out[0], i * NB, NB), stage[:, 2:4, :]).then_inc(f2_out, 16)

            stream(p_f2, lambda i: None,
                   lambda i, p: store_out(i - 1) if p == 2 and not (isinstance(i, int) and i == 0) else None)
            store_out(p_f2.n - 1)
            act.wait_ge(f2_out, 16 * p_f2.n)

        @block.vector
        def _(dve):
            nc.vector.memset(ones[:, :], 1.0).then_inc(consts, 1)
            nc.vector.memset(stat[:, 15:16], EPS).then_inc(consts, 1)
            dve.wait_ge(c_silu, 2)
            nc.vector.tensor_scalar(aneg[:, :], aneg[:, :], -1.0, None, ALU.mult).then_inc(cols_ready, 1)
            dve.wait_ge(vec_T, 1)
            nc.vector.tensor_copy(b_col[:, :], PS[:, 4, 0:96]).then_inc(cols_ready, 1)
            nc.vector.tensor_copy(vec_col[:, :], PS[:, 4, 96:176]).then_inc(cols_ready, 1)
            nc.vector.tensor_copy(conv_w[:, :], PS[:, 4, 176:336]).then_inc(cols_ready, 1)
            nc.vector.tensor_copy(c_col[:, :], PS[:, 4, 336:368]).then_inc(cols_ready, 1)

            dve.wait_ge(n_sqrt, 1)
            nc.vector.reciprocal(stat[:, 4:8], stat[:, 4:8]).then_inc(n_rec, 1)
            dve.wait_ge(n_rec, 1)
            for t in range(4):
                nc.vector.tensor_scalar(x_tok[:, t, :], x_tok[:, t, :], stat[:, 4 + t:5 + t], None,
                                        ALU.mult).then_inc(n_mul, 1)

            dve.wait_ge(mod_used, 4 * p_mod.n)
            dve.wait_ge(cols_ready, 5)
            nc.vector.tensor_tensor(mod[:, :, :], PS[:, 6, 0:192].rearrange("p (k w) -> p k w", w=2),
                                    b_col[:, :].unsqueeze(2).to_broadcast([P, 96, 2]), ALU.add).then_inc(mod_ready, 1)
            dve.wait_ge(mod_ready, 1)
            nc.vector.scalar_tensor_tensor(out=s1[:, :, :], in0=mod[:, 16:32, :], scalar=1.0,
                                           in1=vec_col[:, 0:16].unsqueeze(2).to_broadcast([P, KT, 2]),
                                           op0=ALU.add, op1=ALU.mult).then_inc(mod_ready, 1)
            nc.vector.scalar_tensor_tensor(out=s2[:, :], in0=mod[:, 64:80, 0], scalar=1.0, in1=vec_col[:, 16:32],
                                           op0=ALU.add, op1=ALU.mult).then_inc(mod_ready, 1)
            dve.wait_ge(mod_ready, 3)
            low_groups(dve, G_LAT, act1_hi, act1_lo, 0, lambda k: s1[:, k, 0:1], lambda k: mod[:, k, 0:1])
            low_groups(dve, G_CTX, act1_hi, act1_lo, 16, lambda k: s1[:, k, 1:2], lambda k: mod[:, k, 1:2])

            def low(ph, i, p):
                dve.wait_ge(hi_ready, lin(col(ph.index, p), i) + 1)
                r, h, o = raw[:, p % RAW, :, :], w_hi[:, p % SPL, :, :].bitcast(F32), w_lo[:, p % SPL, :, :]
                if ph is p_dt:
                    r, h, o = [v.rearrange("p k n -> p (k n)")[:, 0:KT * 64] for v in (r, h, o)]
                nc.vector.tensor_tensor(o, r, h, ALU.subtract).then_inc(lo_ready, 1)

            pending = [lambda: None]

            def stream(ph, evac, after=lambda i, p: None):
                def body(i):
                    for p in range(ph.chunks):
                        low(ph, i, p)
                        if p == 0:
                            if isinstance(i, int) and i == 0:
                                pending[0]()
                            else:
                                evac(i - 1)
                        after(i, p)
                each_block(dve, ph.n, body)
                pending[0] = lambda: evac(ph.n - 1)

            nothing = lambda i: None
            stream(p_kv, nothing)
            stream(p_xb, nothing)
            stream(p_dt, nothing)

            k = [0]

            def step(ins, wait=True):
                k[0] += 1
                ins.then_inc(d_dve, 1)
                if wait:
                    dve.wait_ge(d_dve, k[0])

            dve.wait_ge(n_mul, 4)
            dve.wait_ge(tp_done, G_Y)
            for b in range(4):
                wait_bank(dve, p_dt, 0, b)
                ch = 2 + b if b < 2 else b - 2
                nc.vector.tensor_tensor(dt[:, ch, :], PS[:, b, 0:64], dtb[:, :], ALU.add).then_inc(bank_free, 1)
            dve.wait_ge(d_act, 2)
            step(nc.vector.tensor_scalar(acum[:, :, :], av[:, :, :], 1.0, None, ALU.add))
            step(nc.vector.tensor_scalar(eacum[:, :, :], acum[:, :, :], -1.0, None, ALU.add))
            step(nc.vector.tensor_tensor(eacum[:, :, :], av[:, :, :], eacum[:, :, :], ALU.subtract))
            step(nc.vector.reciprocal(wdec[:, :, :], acum[:, :, :]))
            step(nc.vector.tensor_tensor(eacum[:, :, :], eacum[:, :, :], wdec[:, :, :], ALU.mult))
            dve.wait_ge(d_act, 3)
            step(nc.vector.scalar_tensor_tensor(out=dt[:, :, :], in0=dt[:, :, :], scalar=0.0, in1=etot[:, :, :],
                                                op0=ALU.max, op1=ALU.add))
            step(nc.vector.tensor_tensor(dt[:, :, :], dt[:, :, :], eacum[:, :, :], ALU.add))
            step(nc.vector.tensor_tensor(av[:, :, :], dt[:, :, :],
                                         aneg[:, :].unsqueeze(1).to_broadcast([P, 4, 64]), ALU.mult))
            assert k[0] == D_A
            dve.wait_ge(d_pe, 1)
            step(nc.vector.tensor_copy(acum[:, :, :].rearrange("p a b -> p (a b)"), PS[:, 7, 0:256]))
            step(nc.vector.tensor_tensor(wdec[:, :, :].rearrange("p a b -> p (a b)"), PS[:, 7, 256:512],
                                         acum[:, :, :].rearrange("p a b -> p (a b)"), ALU.subtract))
            dve.wait_ge(d_act, 6)
            step(nc.vector.tensor_tensor(wdec[:, :, :], wdec[:, :, :], dt[:, :, :], ALU.mult))
            step(nc.vector.tensor_tensor(wdec[:, 0, 0:32], wdec[:, 0, 0:32], etot[:, 1, 0:32], ALU.mult))
            step(nc.vector.tensor_tensor(wdec[:, 1, 32:64], wdec[:, 1, 32:64], etot[:, 0, 32:64], ALU.mult))
            assert k[0] == D_END
            pending[0] = lambda: None
            stream(p_q, nothing)
            stream(p_c, nothing)

            def rope_tables():
                dve.wait_ge(r_in, 16 * 7)
                nc.vector.tensor_scalar(gain5[:, 0:4, :], gain5[:, 0:4, :], float(AD) ** -0.5, None,
                                        ALU.mult).then_inc(r_dve, 1)
                dve.wait_ge(r_dve, 1)
                for t in range(2):
                    nc.vector.tensor_tensor(cos5[:, t, :, :], gain5[:, :, :],
                                            rope[:, t, 0, :].unsqueeze(1).to_broadcast([P, 5, AD]), ALU.mult)
                    g = gain5[:, :, :].rearrange("p h (a b f) -> p h a b f", a=2, b=2)
                    s = rope[:, t, 1, :].rearrange("p (a b f) -> p a b f", a=2, b=2)
                    o = sin5[:, t, :, :].rearrange("p h (a b f) -> p h a b f", a=2, b=2)
                    for b in range(2):
                        last = nc.vector.tensor_tensor(o[:, :, :, b, :], g[:, :, :, 1 - b, :],
                                                       s[:, :, b, :].unsqueeze(1).to_broadcast([P, 5, 2, 32]), ALU.mult)
                last.then_inc(r_dve, 1)
                dve.wait_ge(r_dve, 2)

            def attention_start(i):
                dve.wait_ge(a_in, i * 80 + 80)
                if isinstance(i, int) and i == 0:
                    rope_tables()
                else:
                    dve.wait_ge(a_qkT, i * 1)
                n = i * 4
                nc.vector.tensor_tensor(qk_sq[:, :, :], qk[:, :, :], qk[:, :, :], ALU.mult).then_inc(a_dve, 1)
                dve.wait_ge(a_dve, n + 1)
                nc.vector.tensor_reduce(ast[:, 0:12], qk_sq[:, :, :], AX_X, ALU.add).then_inc(a_ssq, 1)
                dve.wait_ge(a_sqrt, i + 1)
                nc.vector.reciprocal(ast[:, 24:36], ast[:, 12:24]).then_inc(a_dve, 1)
                dve.wait_ge(a_dve, n + 2)
                nc.vector.tensor_tensor(qk[:, :, :], qk[:, :, :], ast[:, 24:36].unsqueeze(2).to_broadcast([P, 12, AD]),
                                        ALU.mult).then_inc(a_dve, 1)
                dve.wait_ge(a_dve, n + 3)
                def halves(v):
                    return v.rearrange("p h (a b f) -> p (h a) b f", a=2, b=2)
                src, swp = halves(qk[:, 0:10, :]), halves(qk_sq[:, 0:10, :])
                sn = sin5[:, :, :, :].rearrange("p t h (a b f) -> p (t h a) b f", a=2, b=2)
                nc.vector.tensor_tensor(swp[:, :, 0, :], src[:, :, 1, :], sn[:, :, 0, :], ALU.mult)
                nc.vector.tensor_tensor(swp[:, :, 1, :], src[:, :, 0, :], sn[:, :, 1, :], ALU.mult)
                nc.vector.tensor_tensor(qk_r[:, :, :], qk[:, 0:10, :],
                                        cos5[:, :, :, :].rearrange("p t h d -> p (t h) d"), ALU.mult)
                nc.vector.tensor_tensor(qk[:, 10:12, :], qk[:, 10:12, :],
                                        gain5[:, 4:5, :].to_broadcast([P, 2, AD]), ALU.mult).then_inc(a_dve, 1)
                dve.wait_ge(a_dve, n + 4)
                nc.vector.tensor_tensor(qk_r[:, :, :], qk_r[:, :, :], qk_sq[:, 0:10, :], ALU.add).then_inc(a_rope, 1)

            def attention_steps(i, lo, hi):
                for s in range(lo, hi):
                    if s < 8:
                        dve.wait_ge(a_sc, i * 8 + (s + 1))
                        if not (isinstance(i, int) and i == 0 and s < 2):
                            dve.wait_ge(a_exp, i * 8 + (s - 1))
                        nc.vector.tensor_reduce(ast[:, 36 + s % 2:37 + s % 2], PS[:, 2 + s % 2, :], AX_X, ALU.max,
                                                negate=True).then_inc(a_max, 1)
                    if 1 <= s <= 8:
                        u = s - 1
                        dve.wait_ge(a_exp, i * 8 + (u + 1))
                        nc.vector.reciprocal(ast[:, 44 + u % 2:45 + u % 2], ast[:, 40 + u % 2:41 + u % 2]).then_inc(a_rec, 1)
                        dve.wait_ge(a_rec, i * 8 + (u + 1))
                        nc.vector.tensor_scalar(probs[:, u % 2, :], probs[:, u % 2, :], ast[:, 44 + u % 2:45 + u % 2],
                                                None, ALU.mult).then_inc(a_norm, 1)
                    if s >= 4 and s % 2 == 0:
                        h = (s - 4) // 2
                        dve.wait_ge(a_ohi, i * REP + (h + 1))
                        nc.vector.tensor_tensor(act1_lo[:, bass.ds(i * REP + (16 + h), 1), :],
                                                PS[:, 6 + h % 2, 0:T].unsqueeze(1),
                                                act1_hi[:, bass.ds(i * REP + (16 + h), 1), :].bitcast(F32),
                                                ALU.subtract).then_inc(a_o, 1)

            def z_after(i, p):
                if p == 0:
                    attention_start(i)
                attention_steps(i, *((0, 2), (2, 5), (5, 8), (8, 11))[p])

            stream(p_z, nothing, z_after)

            def heads(v, d, g):
                return v[..., bass.ds(g * HPG + d * 32, HPG)]

            def g_after(g, p):
                if p == 0:
                    if isinstance(g, int) and g == 0:
                        dve.wait_ge(a_pv, AH)
                        dve.wait_ge(a_ohi, AH)
                        nc.vector.tensor_scalar(negm[:, :, :], tri[:, :, :], -1.0, 1e30, ALU.add,
                                                ALU.mult).then_inc(s_neg, 1)
                    for d in range(2):
                        ins = nc.vector.tensor_copy(a_loc[:, :, d, :], heads(av[:, 2:4, :], d, g))
                    ins.then_inc(s_loc, 1)
                    dve.wait_ge(s_cin, g + 1)
                    for tap in range(TAPS):
                        if tap:
                            dve.wait_ge(s_tap, g * TAPS + tap)
                        for m in range(7):
                            tile = g * 2 + (32 * tap + m % 4) if m % 4 < 2 else g + (32 * tap + (16 if m % 4 == 2 else 24))
                            w = conv_w[:, bass.ds(tile, 1)]
                            src = cin[:, m, tap:tap + T]
                            if tap == 0:
                                ins = nc.vector.tensor_scalar(cv[:, m, :], src, w, None, ALU.mult)
                            else:
                                ins = nc.vector.scalar_tensor_tensor(out=cv[:, m, :], in0=src, scalar=w, in1=cv[:, m, :],
                                                                     op0=ALU.mult, op1=ALU.add)
                        ins.then_inc(s_tap, 1)
                if p == 1:
                    dve.wait_ge(s_tok, g + 1)
                    x_l = tokb[:, 2:4, 0:256].rearrange("p c (h n) -> p c h n", h=HPG)

                    def weigh(o, x, w, n):
                        return nc.vector.tensor_tensor(o.rearrange("p c (h n) -> p c h n", h=HPG), x,
                                                       w.unsqueeze(3).to_broadcast([P, n, HPG, HD]), ALU.mult)
                    for d in range(2):
                        weigh(xdt[:, d, :, :], x_l, heads(dt[:, 2:4, :], d, g), 2)
                    x_f = tokb[:, 0:3, 0:256].rearrange("p c (h n) -> p c h n", h=HPG)
                    weigh(xdf, x_f, heads(wdec[:, 0:3, :], 0, g), 3)
                    weigh(xdb[:, 0:2, :], x_f[:, 0:2, :, :], heads(wdec[:, 0:2, :], 1, g), 2)
                    weigh(xdb[:, 2:3, :], x_l[:, 1:2, :, :], heads(wdec[:, 3:4, :], 1, g), 1).then_inc(s_xw, 1)
                    dve.wait_ge(s_dc, g + 1)
                    for c in range(2):
                        for d in range(2):
                            nc.vector.tensor_tensor(
                                dec[:, 2 * c + d, :, :], PS[:, 2 + 2 * c + d, :].rearrange("p (h l) -> p h l", h=HPG),
                                heads(acum[:, 2 + c, :], d, g).unsqueeze(2).to_broadcast([P, HPG, P]),
                                ALU.subtract).then_inc(s_D, 1)
                if p == 2:
                    dve.wait_ge(s_E, g + 1)
                    dve.wait_ge(s_cb, g + 1)
                    for c in range(2):
                        v = dec[:, 2 * c:2 * c + 2, :, :].rearrange("p d h l -> p (d h) l")
                        ins = nc.vector.tensor_tensor(
                            v, v, PS[:, 6, c * P:(c + 1) * P].unsqueeze(1).to_broadcast([P, 2 * HPG, P]), ALU.mult)
                    ins.then_inc(s_M, 1)
                    dve.wait_ge(s_h0, g + 1)
                    for o, src, ch, d in ((hst[:, 1, 0, :], hst[:, 0, 0, :], 2, 0), (hst[:, 0, 1, :], hst[:, 1, 1, :], 3, 1)):
                        ins = nc.vector.tensor_tensor(o.rearrange("p (h n) -> p h n", h=HPG),
                                                      src.rearrange("p (h n) -> p h n", h=HPG),
                                                      heads(etot[:, ch, :], d, g).unsqueeze(2).to_broadcast([P, HPG, HD]),
                                                      ALU.mult)
                    ins.then_inc(s_ht, 1)
                    dve.wait_ge(s_ht, g + 1)
                    dve.wait_ge(s_S, g + 1)
                    nc.vector.tensor_tensor(hst[:, 1, 0, :], hst[:, 1, 0, :], PS[:, 2, 0:256], ALU.add)
                    nc.vector.tensor_tensor(hst[:, 0, 1, :], hst[:, 0, 1, :], PS[:, 2, 256:512], ALU.add).then_inc(s_h1, 1)
                if p == 3:
                    dve.wait_ge(s_yo, g + 1)
                    dve.wait_ge(s_yd, g + 1)
                    for c in range(2):
                        w = eacum[:, 2 + c, :].rearrange("p (d h) -> p d h", d=2)[:, :, bass.ds(g * HPG, HPG)]
                        nc.vector.tensor_tensor(yt[:, c, :].rearrange("p (d h n) -> p d h n", d=2, h=HPG),
                                                PS[:, 3 + c, :].rearrange("p (d h n) -> p d h n", d=2, h=HPG),
                                                w.unsqueeze(3).to_broadcast([P, 2, HPG, HD]), ALU.mult)
                    nc.vector.tensor_tensor(yx.rearrange("p c (h n) -> p c h n", h=HPG),
                                            tokb[:, 2:4, 0:256].rearrange("p c (h n) -> p c h n", h=HPG),
                                            dskip[:, bass.ds(g * HPG, HPG)].unsqueeze(1).unsqueeze(3)
                                            .to_broadcast([P, 2, HPG, HD]), ALU.mult).then_inc(s_y1, 1)
                    dve.wait_ge(s_y1, g + 1)
                    if not (isinstance(g, int) and g == 0):
                        dve.wait_ge(s_yst, g * 16)
                    nc.vector.tensor_tensor(yb[:, :, :], yt[:, :, 0:256], yt[:, :, 256:512], ALU.add)
                    nc.vector.tensor_tensor(yx, yx, PS[:, 5, :].rearrange("p (c n) -> p c n", c=2),
                                            ALU.add).then_inc(s_y2, 1)
                    dve.wait_ge(s_y2, g + 1)
                    nc.vector.tensor_tensor(yb[:, :, :], yb[:, :, :], yx, ALU.add).then_inc(s_y3, 1)
                    dve.wait_ge(s_y3, g + 1)
                    dve.wait_ge(s_zs, g + 1)
                    nc.vector.tensor_tensor(yb[:, :, :], yb[:, :, :], zt[:, :, :], ALU.mult).then_inc(s_yz, 1)
                    dve.wait_ge(s_sq, g + 1)
                    nc.vector.reciprocal(sst[:, 4:6], sst[:, 2:4]).then_inc(s_rec, 1)
                    dve.wait_ge(s_rec, g + 1)
                    dve.wait_ge(s_yz, g + 1)
                    for c in range(2):
                        ins = nc.vector.tensor_scalar(yb[:, c, :], yb[:, c, :], sst[:, 4 + c:5 + c], None, ALU.mult)
                    ins.then_inc(s_y, 1)

            stream(p_g, nothing, g_after)
            low_groups(dve, G_Y, act1_hi, act1_lo, 0, lambda k: vec_col[:, 32 + k:33 + k], None)

            def merge(i):
                dve.wait_ge(g_sig, i + 1)
                if not (isinstance(i, int) and i == 0):
                    dve.wait_ge(g_ev, i * 1)
                for b in range(4):
                    wait_bank(dve, p_br, i, b)
                    t, br = b % 2, b // 2
                    dst = wide[:, t, bass.ts(i, NB)] if br == 0 else tmp[:, t, :, :].rearrange("p a b -> p (a b)")
                    nc.vector.tensor_tensor(dst, PS[:, b, :], gates[:, br, t, :], ALU.mult).then_inc(bank_free, 1)
                dve.wait_ge(bank_free, lin(p_br.bank0, i) + 4)
                ins = nc.vector.tensor_tensor(wide[:, :, bass.ts(i, NB)], wide[:, :, bass.ts(i, NB)],
                                              tmp[:, :, :, :].rearrange("p t a b -> p t (a b)"), ALU.add)
                ins.then_inc(g_ev, 1)

            stream(p_br, merge)
            pending[0]()
            for m in range(8):
                if m >= 1:
                    dve.wait_ge(dg_T, m)
                for j in range(4):
                    kcol = (32 if m < 4 else 80) + (m % 4) * 4 + j
                    ins = nc.vector.tensor_scalar(diag[:, j, :], ident[:, :], mod[:, kcol, 0:1], None, ALU.mult)
                ins.then_inc(dg_ready, 1)
                if m == 3:
                    low_groups(dve, G_M, act1_hi, act1_lo, 0, None, None)

            def residual(i):
                if isinstance(i, int) and i == 0:
                    dve.wait_ge(xres_in, 16)
                    dve.wait_ge(gt_ready, 4)
                else:
                    dve.wait_ge(o_ev, i * 1)
                for t in range(2):
                    wait_bank(dve, p_o, i, t)
                    nc.vector.tensor_tensor(tmp[:, t, :, :].rearrange("p a b -> p (a b)"), PS[:, t, :],
                                            gt1[:, bass.ts(i, NB)], ALU.mult).then_inc(bank_free, 1)
                dve.wait_ge(bank_free, lin(p_o.bank0, i) + 2)
                nc.vector.tensor_tensor(xres[:, :, bass.ts(i, NB)], xres[:, :, bass.ts(i, NB)],
                                        tmp[:, :, :, :].rearrange("p t a b -> p t (a b)"), ALU.add).then_inc(o_ev, 1)

            pending[0] = lambda: None
            stream(p_o, residual)
            pending[0]()
            dve.wait_ge(n_sqrt, 2)
            nc.vector.reciprocal(stat[:, 10:12], stat[:, 10:12]).then_inc(n_rec, 1)
            dve.wait_ge(n_rec, 2)
            dve.wait_ge(xm_out, 16)
            for t in range(2):
                nc.vector.tensor_scalar(wide[:, t, :], xres[:, t, :], stat[:, 10 + t:11 + t], None,
                                        ALU.mult).then_inc(n_mul, 1)
            dve.wait_ge(xm_out, 32)
            low_groups(dve, G_H2, act2_hi, act2_lo, H2, lambda k: s2[:, k:k + 1], lambda k: mod[:, 48 + k, 0:1])

            def hidden(i):
                for t in range(2):
                    wait_bank(dve, p_f1, i, 2 + t)
                    dve.wait_ge(bank_free, lin(p_f1.bank0, i) + 2)
                    nc.vector.tensor_tensor(stage[:, t, :], stage[:, t, :], PS[:, 2 + t, :], ALU.mult).then_inc(bank_free, 1)

            def hidden_low(i):
                dve.wait_ge(f_hi, i + 1)
                nc.vector.tensor_tensor(
                    act2_lo[:, bass.ds(i * 4, 4), :].rearrange("p (b k) t -> p b (k t)", b=2), PS[:, 4:6, :],
                    act2_hi[:, bass.ds(i * 4, 4), :].bitcast(F32).rearrange("p (b k) t -> p b (k t)", b=2),
                    ALU.subtract).then_inc(f_lo, 1)

            def f1_after(i, p):
                if p == 2 and not (isinstance(i, int) and i == 0):
                    hidden_low(i - 1)

            pending[0] = lambda: None
            stream(p_f1, hidden, f1_after)
            pending[0] = lambda: (hidden(p_f1.n - 1), hidden_low(p_f1.n - 1))

            def finish(i):
                dve.wait_ge(f2_in, i * 32 + 32)
                if not (isinstance(i, int) and i == 0):
                    dve.wait_ge(f2_out, i * 16)
                for t in range(2):
                    wait_bank(dve, p_f2, i, t)
                    nc.vector.tensor_tensor(stage[:, 2 + t, :], PS[:, t, :], tmp[:, 0, :, :].rearrange("p a b -> p (a b)"),
                                            ALU.mult).then_inc(bank_free, 1)
                dve.wait_ge(bank_free, lin(p_f2.bank0, i) + 2)
                nc.vector.tensor_tensor(stage[:, 2:4, :], stage[:, 2:4, :], stage[:, 0:2, :], ALU.add).then_inc(f2_ev, 1)

            stream(p_f2, finish)
            pending[0]()


SETUP = 15
D_A = 8
D_END = D_A + 5
NAMES = ["x", "c", "ctx", "c_ctx", "w_mod", "b_mod", "norm1", "w_in", "conv_w", "conv_b", "dt_bias", "a_log",
         "d_skip", "ssm_norm", "q_norm", "k_norm", "w_ssm_br", "w_attn_br", "w_o", "norm2", "w_ffn_in", "w_ffn_out"]


def shape_constants():
    pos = np.arange(T)
    n = AD // 4
    inv = np.power(np.float32(THETA), -np.arange(n, dtype=np.float32) / np.float32(n)).astype(np.float32)
    ang = np.stack([(pos // GRID_W).astype(np.float32)[:, None] * inv,
                    (pos % GRID_W).astype(np.float32)[:, None] * inv], axis=1)
    cos, sin = np.cos(ang).astype(np.float32), np.sin(ang).astype(np.float32)
    return {
        "c_ident": np.eye(P, dtype=np.float32),
        "c_tri_f": np.triu(np.ones((P, P), np.float32)),
        "c_tri_b": np.tril(np.ones((P, P), np.float32)),
        "rope_cos": np.ascontiguousarray(np.stack([cos, cos], axis=2).reshape(T, AD)),
        "rope_sin": np.ascontiguousarray(np.stack([-sin, sin], axis=2).reshape(T, AD)),
    }


def kernel(**inputs):
    import concourse.bacc as bacc
    from concourse.bass_utils import run_bass_kernel_spmd

    nc = bacc.Bacc("TRN2", target_bir_lowering=False, num_devices=1)
    arrays, aps = {}, {}
    for name, value in [(n, inputs[n]) for n in NAMES] + list(shape_constants().items()):
        value = np.ascontiguousarray(value)
        arrays[f"in_{name}"] = value
        aps[name] = nc.dram_tensor(f"in_{name}", value.shape, mybir.dt.from_np(value.dtype), kind="ExternalInput").ap()
    out = nc.dram_tensor("out_x", (1, T, D), F32, kind="ExternalOutput").ap()
    hybrid_block(nc, aps, out)
    r = run_bass_kernel_spmd(nc, [arrays], core_ids=[0])
    return r.results[0]["out_x"]
```

```python
from contextlib import ExitStack

import numpy as np

import concourse.bass as bass
from concourse import mybir

F32 = mybir.dt.float32
F32R = mybir.dt.float32r
ALU = mybir.AluOpType
ACT = mybir.ActivationFunctionType
AX_X = mybir.AxisListType.X

P = 128
D = 2048
T = 256
TT = T // P
KT = D // P
HEADS, HD = 32, 64
GROUPS, NST = 8, 128
HPG = HEADS // GROUPS
TAPS = 5
AH, KVH, AD = 16, 4, 128
REP = AH // KVH
DFF = 5632
FT = DFF // P
GRID_W, THETA = 64, 10000.0
EPS = 1e-6
CZ, CX, CB, CC, CDT = 0, 2048, 4096, 5120, 6144
CQ, CK, CV, CG = 6208, 8256, 8768, 9280
DIN = 13376
NB = 512
CK_T = 4
RAW, SPL = 4, 2


class Phase:

    def __init__(self, name, n, chunks, kind, tiles, banks, staged=False):
        self.name, self.n, self.chunks, self.kind = name, n, chunks, kind
        self.tiles, self.banks, self.staged = tiles, banks, staged


def plan(phases):
    raw_user = [None] * RAW
    spl_user = [None] * SPL
    loads = [0] * RAW
    count = {"mod": 0, "split": 0}
    banks = done = 0
    staged = [0] * 4
    for ph in phases:
        ph.loaded, ph.raw_prev, ph.index, ph.spl_prev = [], [], [], []
        ph.bank0, ph.done0, ph.stage0 = [], [], []
        for _ in range(ph.n):
            ph.bank0.append(banks)
            ph.done0.append(done)
            ph.stage0.append(list(staged))
            banks += len(ph.banks)
            done += len(ph.banks) - len(ph.banks) // max(1, len(ph.tiles))
            if ph.staged:
                for b in range(len(ph.banks)):
                    staged[b] += 16
            row = [[], [], [], []]
            for p in range(ph.chunks):
                s = p % RAW
                loads[s] += 1
                row[0].append(loads[s] * 16)
                row[1].append(raw_user[s])
                row[2].append(count[ph.kind])
                raw_user[s] = (ph.kind, count[ph.kind])
                if ph.kind == "split":
                    row[3].append(spl_user[p % SPL])
                    spl_user[p % SPL] = count["split"]
                else:
                    row[3].append(None)
                count[ph.kind] += 1
            for a, b in zip((ph.loaded, ph.raw_prev, ph.index, ph.spl_prev), row):
                a.append(b)
        ph.banks_end, ph.staged_end, ph.count_end = banks, list(staged), dict(count)


def lin(values, i):
    if isinstance(i, int):
        return values[i]
    step = values[2] - values[1]
    assert all(b - a == step for a, b in zip(values[1:], values[2:]))
    return i * step + (values[1] - step)


def each_block(eng, n, body):
    body(0)
    if n == 2:
        body(1)
    elif n > 2:
        with eng.Fori(1, n) as i:
            body(i)


def hybrid_block(nc, a, out):
    with ExitStack() as outer:
        def sem(name):
            return outer.enter_context(nc.semaphore(name))

        def sb(name, shape, dt=F32, scope=outer):
            return scope.enter_context(nc.sbuf_tensor(name, shape, dt))

        def dram(name, shape):
            return nc.dram_tensor(name, shape, F32, kind="Internal").ap()

        proj_lat, proj_ctx = dram("proj_lat", (T, DIN)), dram("proj_ctx", (T, DIN))
        y_dram, xmid_dram, gate2_dram = dram("y_scratch", (T, D)), dram("xmid", (T, D)), dram("gate2", (1, D))

        LAT, BOTH = [0, 1], [0, 1, 2, 3]
        p_mod = Phase("mod", 8, 4, "split", [], [])
        p_kv = Phase("kv", 2, 4, "split", BOTH, BOTH, True)
        p_xb = Phase("xb", 6, 4, "split", BOTH, BOTH, True)
        p_dt = Phase("dt", 1, 1, "split", BOTH, BOTH)
        p_q = Phase("q", 4, 4, "split", LAT, LAT, True)
        p_c = Phase("c", 2, 4, "split", LAT, LAT, True)
        p_z = Phase("z", 4, 12, "split", LAT, LAT, True)
        p_g = Phase("g", 8, 8, "split", LAT, LAT, True)
        ORDER = {"z": ["z0", "m0", "m1", "z1", "m2", "m3", "z2", "m4", "m5", "z3", "m6", "m7"],
                 "g": ["g0", "m0", "g1", "m1", "g2", "m2", "g3", "m3"]}
        p_br = Phase("br", 4, 8, "split", LAT, BOTH)
        p_o = Phase("o", 4, 4, "split", LAT, LAT)
        p_f1 = Phase("f1", DFF // NB, 8, "split", LAT, BOTH)
        p_f2 = Phase("f2", 4, FT // CK_T, "split", LAT, LAT)
        phases = [p_mod, p_kv, p_xb, p_dt, p_q, p_c, p_z, p_g, p_br, p_o, p_f1, p_f2]
        plan(phases)
        PROJ_COL = {"kv": CK, "xb": CX, "q": CQ, "c": CC, "z": CZ, "g": CG}

        def kview(w):
            return w.rearrange("(c k p) n -> c p k n", p=P, k=CK_T)

        w_mod, w_in = kview(a["w_mod"][0]), kview(a["w_in"][0])
        w_sb, w_ab, w_ob = kview(a["w_ssm_br"][0]), kview(a["w_attn_br"][0]), kview(a["w_o"][0])
        w_f1, w_f2 = kview(a["w_ffn_in"][0]), kview(a["w_ffn_out"][0])
        w_dt = a["w_in"][0].rearrange("(k p) n -> p k n", p=P)[:, :, CDT:CDT + 64]
        x_in = a["x"][0].rearrange("(t p) n -> p t n", p=P)
        ctx_in = a["ctx"][0].rearrange("(t p) n -> p t n", p=P)

        def source(ph, i, p):
            if ph is p_mod:
                return w_mod[p, :, :, bass.ts(i, NB)]
            if ph.name in ORDER:
                what, q = ORDER[ph.name][p][0], int(ORDER[ph.name][p][1])
                if what == "m":
                    first = (i * 2 + (8 + q // 4)) if ph is p_z else i + 16
                    return w_mod[q % 4, :, :, bass.ds(first * NB, NB)]
                p = q
            if ph.name in PROJ_COL:
                return w_in[p, :, :, bass.ds(i * NB + PROJ_COL[ph.name], NB)]
            if ph is p_br:
                return (w_ab if p < 4 else w_sb)[p % 4, :, :, bass.ts(i, NB)]
            if ph is p_o:
                return w_ob[p, :, :, bass.ts(i, NB)]
            if ph is p_f1:
                return w_f1[p % 4, :, :, bass.ds(i * NB + (p // 4) * DFF, NB)]
            return w_f2[p, :, :, bass.ts(i, NB)]

        PS = outer.enter_context(nc.psum_tensor("PS", [P, 8, NB], F32))
        raw = sb("raw", [P, RAW, CK_T, NB])
        w_hi = sb("w_hi", [P, SPL, CK_T, NB], F32R)
        w_lo = sb("w_lo", [P, SPL, CK_T, NB], F32R)
        ident = sb("ident", [P, P])
        ones = sb("ones", [P, P])
        tri = sb("tri", [P, 2, P])
        m2 = sb("m2", [P, 8])
        mod = sb("mod", [P, 96, 2])
        b_col = sb("b_col", [P, 96])
        vec_col = sb("vec_col", [P, 80])
        conv_w = sb("conv_w", [P, TAPS * 32])
        s1 = sb("s1", [P, KT, 2])
        s2 = sb("s2", [P, KT])
        tmp = sb("tmp", [P, 2, 2, T])
        stage = sb("stage", [P, 4, NB])
        stat = sb("stat", [P, 16])
        dskip = sb("dskip", [P, HEADS])
        dtb = sb("dtb", [P, 64])
        aneg = sb("aneg", [P, 64])
        junk = stage[:, :, :].rearrange("p a b -> p (a b)")

        s_A = ExitStack()
        act1_hi = sb("act1_hi", [P, 32, T], F32R, s_A)
        act1_lo = sb("act1_lo", [P, 32, T], F32R, s_A)
        c4 = sb("c4", [P, KT, P], F32R, s_A)
        res4 = sb("res4", [P, NB], F32, s_A)
        s_0 = ExitStack()
        x_tok = sb("x_tok", [P, 4, D], F32, s_0)
        rows = sb("rows", [P, 4, P], F32, s_0)
        c_rows = sb("c_rows", [32, P], F32, s_0)
        c_col = sb("c_col", [P, 2 * KT], F32, s_0)
        s_0.close()
        s_1 = ExitStack()
        dt = sb("dt", [P, 4, 64], F32, s_1)
        av = sb("av", [P, 4, 64], F32, s_1)
        acum = sb("acum", [P, 4, 64], F32, s_1)
        etot = sb("etot", [P, 4, 64], F32, s_1)
        eacum = sb("eacum", [P, 4, 64], F32, s_1)
        wdec = sb("wdec", [P, 4, 64], F32, s_1)
        s_2 = ExitStack()
        gain_k = sb("gain_k", [P, AD], F32, s_2)
        cos5 = sb("cos5", [P, 2, 5, AD], F32, s_2)
        sin5 = sb("sin5", [P, 2, 5, AD], F32, s_2)
        qk = sb("qk", [P, 12, AD], F32, s_2)
        qk_sq = sb("qk_sq", [P, 12, AD], F32, s_2)
        qk_r = sb("qk_r", [P, 10, AD], F32, s_2)
        vv = sb("vv", [P, 4, AD], F32, s_2)
        kT = sb("kT", [P, 2 * T], F32, s_2)
        probs = sb("probs", [P, 2, 2 * T], F32, s_2)
        pT = sb("pT", [P, 2, 4, T], F32, s_2)
        ast = sb("ast", [P, 64], F32, s_2)
        s_2.close()
        s_3 = ExitStack()
        negm = sb("negm", [P, 2, P], F32, s_3)
        a_loc = sb("a_loc", [P, 2, 2, HPG], F32, s_3)
        u_lat = sb("u_lat", [P, 2, 512], F32, s_3)
        u_ctx = sb("u_ctx", [P, 2, 384], F32, s_3)
        cin = sb("cin", [P, 7, T + 4], F32, s_3)
        cv = sb("cv", [P, 7, T], F32, s_3)
        tokb = sb("tokb", [P, 4, 384], F32, s_3)
        dec = sb("dec", [P, 4, HPG, P], F32, s_3)
        hst = sb("hst", [P, 2, 2, 256], F32, s_3)
        yb = sb("yb", [P, 2, 256], F32, s_3)
        zt = sb("zt", [P, 2, 256], F32, s_3)
        sst = sb("sst", [P, 8], F32, s_3)
        s_3.close()
        s_1.close()
        s_4 = ExitStack()
        wide = sb("wide", [P, 2, D], F32, s_4)
        gates = sb("gates", [P, 2, 2, NB], F32, s_4)
        xres = sb("xres", [P, 2, D], F32, s_4)
        gt1 = sb("gt1", [P, D], F32, s_4)
        diag = sb("diag", [P, 4, P], F32, s_4)
        g2t = sb("g2t", [P, NB], F32, s_4)
        s_4.close()
        s_A.close()
        act2_hi = sb("act2_hi", [P, 60, T], F32R)
        act2_lo = sb("act2_lo", [P, 60, T], F32R)
        H2 = FT
        qT = tmp[:, :, :, :].rearrange("p a b t -> p (a b) t")
        gain5 = probs[:, :, :].rearrange("p a b -> p (a b)")[:, 0:5 * AD].rearrange("p (h n) -> p h n", h=5)
        rope = kT[:, :].rearrange("p (t s n) -> p t s n", t=2, s=2)
        xdt = tmp
        xdf, xdb = cin[:, 0:3, 2:2 + T], cin[:, 3:6, 2:2 + T]
        yt = dec[:, :, :, :].rearrange("p c h l -> p (c h l)")[:, 0:1024].rearrange("p (c n) -> p c n", c=2)
        yx = cv[:, 4:6, :]

        setup_in, x_loaded, c_silu, vec_T, cols_ready = map(sem, (
            "setup_in", "x_loaded", "c_silu", "vec_T", "cols_ready"))
        raw_loaded = [sem(f"raw_loaded{s}") for s in range(RAW)]
        c_split, m_copied, m_T, m_red, mod_ready, s1_ready, s2_ready = map(sem, (
            "c_split", "m_copied", "m_T", "m_red", "mod_ready", "s1_ready", "s2_ready"))
        hi_ready, lo_ready, pe_used = sem("hi_ready"), sem("lo_ready"), sem("pe_used")
        bank_done, bank_free = sem("bank_done"), sem("bank_free")
        stored = [sem(f"stored{s}") for s in range(4)]
        n_sq, n_sqrt, n_rec, n_mul = sem("n_sq"), sem("n_sqrt"), sem("n_rec"), sem("n_mul")
        tp_done, tp_tmp, tp_hi, tp_lo = sem("tp_done"), sem("tp_tmp"), sem("tp_hi"), sem("tp_lo")
        consts = sem("consts")
        d_dve, d_act, d_pe = sem("d_dve"), sem("d_act"), sem("d_pe")
        r_in, r_dve = sem("r_in"), sem("r_dve")
        (a_in, a_vin, a_dve, a_ssq, a_sqrt, a_rope, a_qkT, a_qkS, a_sc, a_max, a_exp, a_rec, a_norm, a_pT,
         a_pTs, a_pv, a_ohi, a_o) = map(sem, (
             "a_in", "a_vin", "a_dve", "a_ssq", "a_sqrt", "a_rope", "a_qkT", "a_qkS", "a_sc", "a_max", "a_exp",
             "a_rec", "a_norm", "a_pT", "a_pTs", "a_pv", "a_ohi", "a_o"))
        s_neg = sem("s_neg")
        (s_pre, s_in, s_zin, s_loc, s_Tin, s_cin, s_tap, s_silu, s_zs, s_Tb, s_cb, s_tok, s_dc, s_D, s_E, s_xw,
         s_H, s_S, s_M, s_h0, s_ht, s_h1, s_yo, s_yd, s_y1, s_y2, s_y3, s_yz, s_sqa, s_sq, s_rec, s_y,
         s_yst) = map(sem, (
             "s_pre", "s_in", "s_zin", "s_loc", "s_Tin", "s_cin", "s_tap", "s_silu", "s_zs", "s_Tb", "s_cb",
             "s_tok", "s_dc", "s_D", "s_E", "s_xw", "s_H", "s_S", "s_M", "s_h0", "s_ht", "s_h1", "s_yo", "s_yd",
             "s_y1", "s_y2", "s_y3", "s_yz", "s_sqa", "s_sq", "s_rec", "s_y", "s_yst"))
        y_in, xres_in, g_in, g_sig, g_tmp, g_ev = map(sem, ("y_in", "xres_in", "g_in", "g_sig", "g_tmp", "g_ev"))
        dg_ready, dg_T, gt_ready, o_tmp, o_ev = map(sem, ("dg_ready", "dg_T", "gt_ready", "o_tmp", "o_ev"))
        g2_out = sem("g2_out")
        xm_out, f_T, f_hi, f_lo = map(sem, ("xm_out", "f_T", "f_hi", "f_lo"))
        f2_in, f2_tmp, f2_ev, f2_out = map(sem, ("f2_in", "f2_tmp", "f2_ev", "f2_out"))

        block = outer.enter_context(nc.Block())

        def rows2(view, c0, n):
            return view.rearrange("(t p) n -> p t n", p=P)[:, :, bass.ds(c0, n)]

        def col(table, p):
            return [row[p] for row in table]

        def last_chunk(ph, b):
            if ph.name in ORDER:
                return ORDER[ph.name].index(ph.name + "3")
            return 4 * (b // 2) + 3 if len(ph.banks) > len(ph.tiles) else ph.chunks - 1

        def wait_bank(eng, ph, i, b):
            if b % len(ph.tiles) == len(ph.tiles) - 1:
                eng.wait_ge(pe_used, lin(col(ph.index, last_chunk(ph, b)), i) + 1)
            else:
                before = b // len(ph.tiles) * (len(ph.tiles) - 1) + b % len(ph.tiles)
                eng.wait_ge(bank_done, lin(ph.done0, i) + before + 1)

        def wait_split_slot(eng, ph, i, p):
            prev = col(ph.spl_prev, p)
            if isinstance(i, int):
                if prev[i] is not None:
                    eng.wait_ge(pe_used, prev[i] + 1)
            else:
                eng.wait_ge(pe_used, lin(prev, i) + 1)

        G_LAT, G_CTX, G_Y, G_M, G_H2 = 0, 8, 16, 24, 32

        def transpose_groups(pe, first, rows_of, ms=range(8)):
            for m in ms:
                g = first + m
                if g >= 2:
                    pe.wait_ge(tp_tmp, g - 1)
                for k in range(2):
                    for t in range(2):
                        last = nc.tensor.transpose(PS[:, 4 + g % 2, k * T + t * P:k * T + (t + 1) * P],
                                                   rows_of(t, 2 * m + k), ident[:, :])
                last.then_inc(tp_done, 1)

        def high_groups(act, first, hi, k0, ms=range(8)):
            for m in ms:
                g = first + m
                act.wait_ge(tp_tmp, g + 1)
                nc.scalar.activation(hi[:, k0 + 2 * m:k0 + 2 * m + 2, :], tmp[:, g % 2, :, :],
                                     ACT.Copy).then_inc(tp_hi, 1)

        def low_groups(dve, first, hi, lo, k0, scale, shift, ms=range(8)):
            def copy_out(m):
                g = first + m
                dve.wait_ge(tp_done, g + 1)
                if g >= 2:
                    dve.wait_ge(tp_hi, g - 1)
                    dve.wait_ge(tp_lo, g - 1)
                for k in range(2):
                    src = PS[:, 4 + g % 2, k * T:(k + 1) * T]
                    dst = tmp[:, g % 2, k, :]
                    if shift is not None:
                        ins = nc.vector.tensor_scalar(dst, src, scale(2 * m + k), shift(2 * m + k), ALU.mult, ALU.add)
                    elif scale is not None:
                        ins = nc.vector.tensor_scalar(dst, src, scale(2 * m + k), None, ALU.mult)
                    else:
                        ins = nc.vector.tensor_copy(dst, src)
                ins.then_inc(tp_tmp, 1)

            def low(m):
                g = first + m
                dve.wait_ge(tp_hi, g + 1)
                dve.wait_ge(tp_tmp, g + 1)
                ks = slice(k0 + 2 * m, k0 + 2 * m + 2)
                nc.vector.tensor_tensor(lo[:, ks, :], tmp[:, g % 2, :, :], hi[:, ks, :].bitcast(F32),
                                        ALU.subtract).then_inc(tp_lo, 1)

            copy_out(ms[0])
            for m in ms:
                if m < ms[-1]:
                    copy_out(m + 1)
                low(m)

        def both_streams(groups, pair):
            groups(0, 2 * pair)
            groups(1, 2 * pair + 2)

        def two_peeled(eng, n, body):
            body(0)
            body(1)
            with eng.Fori(2, n) as i:
                body(i)

        def pipelined(eng, n, body):
            body(0, False)
            with eng.Fori(1, n - 1) as i:
                body(i, False)
            body(n - 1, True)

        @block.sync
        def _(sp):
            def load(ph, i, p):
                prev = col(ph.raw_prev, p)
                s = p % RAW
                user = prev[i if isinstance(i, int) else 1]
                if user is not None:
                    idx = user[1] if isinstance(i, int) else lin([u[1] if u else None for u in prev], i)
                    sp.wait_ge(lo_ready, idx + 1)
                if ph is p_dt:
                    dst = raw[:, s, :, :].rearrange("p k n -> p (k n)")[:, 0:KT * 64].rearrange(
                        "p (k n) -> p k n", n=64)
                    sp.dma_start(dst, w_dt).then_inc(raw_loaded[s], 16)
                else:
                    sp.dma_start(raw[:, s, :, :], source(ph, i, p)).then_inc(raw_loaded[s], 16)

            for ph in phases:
                each_block(sp, ph.n, lambda i: [load(ph, i, p) for p in range(ph.chunks)])

        @block.gpsimd
        def _(pool):
            pool.dma_start(x_tok[:, 0:2, :], x_in).then_inc(x_loaded, 16)
            pool.dma_start(x_tok[:, 2:4, :], ctx_in).then_inc(x_loaded, 16)

            def all_stored(ph):
                for b in range(4):
                    pool.wait_ge(stored[b], ph.staged_end[b])

            all_stored(p_q)
            pool.wait_ge(bank_free, p_q.banks_end)
            pool.wait_ge(n_mul, 4)
            pool.wait_ge(tp_done, G_Y)
            pool.dma_start(rope[:, :, 0, :], a["rope_cos"].rearrange("(t p) n -> p t n", p=P)).then_inc(r_in, 16)
            pool.dma_start(rope[:, :, 1, :], a["rope_sin"].rearrange("(t p) n -> p t n", p=P)).then_inc(r_in, 16)
            for h in range(REP):
                pool.dma_start(gain5[:, h, :], a["q_norm"][0:1, :].to_broadcast([P, AD])).then_inc(r_in, 16)
            pool.dma_start(gain5[:, 4, :], a["k_norm"][0:1, :].to_broadcast([P, AD])).then_inc(r_in, 16)
            pool.dma_start(gain_k[:, :], a["k_norm"][0:1, :].to_broadcast([P, AD])).then_inc(r_in, 16)

            def attention_loads(i):
                if not (isinstance(i, int) and i == 0):
                    pool.wait_ge(a_qkT, i * 1)
                for t in range(2):
                    pool.dma_start(qk[:, 5 * t:5 * t + 4, :], proj_lat[t * P:(t + 1) * P, bass.ds(i * 512 + CQ, 512)]
                                   .rearrange("p (h d) -> p h d", d=AD)).then_inc(a_in, 16)
                    pool.dma_start(qk[:, 5 * t + 4, :], proj_lat[t * P:(t + 1) * P, bass.ds(i * AD + CK, AD)]
                                   ).then_inc(a_in, 16)
                pool.dma_start(qk[:, 10:12, :], rows2(proj_ctx, i * AD + CK, AD)).then_inc(a_in, 16)
                if not (isinstance(i, int) and i == 0):
                    pool.wait_ge(a_pv, i * REP)
                pool.dma_start(vv[:, 0:2, :], rows2(proj_ctx, i * AD + CV, AD)).then_inc(a_vin, 16)
                pool.dma_start(vv[:, 2:4, :], rows2(proj_lat, i * AD + CV, AD)).then_inc(a_vin, 16)

            each_block(pool, KVH, attention_loads)

            all_stored(p_z)
            pool.wait_ge(a_o, AH)
            nc.gpsimd.memset(cin[:, :, 0:2], 0.0)
            nc.gpsimd.memset(cin[:, :, T + 2:T + 4], 0.0).then_inc(s_pre, 1)

            def ssd_loads(g):
                if not (isinstance(g, int) and g == 0):
                    pool.wait_ge(s_Tin, g * 1)
                for view, u, c0, n, o in ((proj_lat, u_lat, g * 256 + CX, 256, 0), (proj_lat, u_lat, g * NST + CB, NST, 256),
                                          (proj_lat, u_lat, g * NST + CC, NST, 384), (proj_ctx, u_ctx, g * 256 + CX, 256, 0),
                                          (proj_ctx, u_ctx, g * NST + CB, NST, 256)):
                    pool.dma_start(u[:, :, o:o + n], rows2(view, c0, n)).then_inc(s_in, 16)
                if not (isinstance(g, int) and g == 0):
                    pool.wait_ge(s_yz, g * 1)
                pool.dma_start(zt[:, :, :], rows2(proj_lat, g * 256 + CZ, 256)).then_inc(s_zin, 16)

            each_block(pool, GROUPS, ssd_loads)

            all_stored(p_g)
            pool.wait_ge(s_yst, 16 * GROUPS)
            pool.dma_start(wide[:, :, :], y_dram.rearrange("(t p) n -> p t n", p=P)).then_inc(y_in, 16)
            pool.dma_start(xres[:, :, :], x_in).then_inc(xres_in, 16)

            def gate_loads(i):
                if not (isinstance(i, int) and i == 0):
                    pool.wait_ge(g_ev, i * 1)
                pool.dma_start(gates[:, 0, :, :], rows2(proj_lat, i * NB + CG + D, NB)).then_inc(g_in, 16)
                pool.dma_start(gates[:, 1, :, :], rows2(proj_lat, i * NB + CG, NB)).then_inc(g_in, 16)

            each_block(pool, 4, gate_loads)
            pool.wait_ge(o_ev, 4)
            pool.dma_start(xmid_dram.rearrange("(t p) n -> p t n", p=P), xres[:, :, :]).then_inc(xm_out, 16)
            pool.wait_ge(xm_out, 16)
            pool.wait_ge(g2_out, 64)
            pool.wait_ge(f_lo, DFF // NB)

            def out_step(i):
                if not (isinstance(i, int) and i == 0):
                    pool.wait_ge(f2_ev, i * 1)
                pool.dma_start(stage[:, 0:2, :], rows2(xmid_dram, i * NB, NB)).then_inc(f2_in, 16)
                pool.dma_start(tmp[:, 0, :, :].rearrange("p a b -> p (a b)"),
                               gate2_dram[:, bass.ts(i, NB)].to_broadcast([P, NB])).then_inc(f2_in, 16)

            each_block(pool, 4, out_step)

        @block.tensor
        def _(pe):
            def chunk(ph, i, p, acts, banks, kt0, first, final):
                pe.wait_ge(hi_ready, lin(col(ph.index, p), i) + 1)
                pe.wait_ge(lo_ready, lin(col(ph.index, p), i) + 1)
                s = p % SPL
                n, ks = (64, KT) if ph is p_dt else (NB, CK_T)
                hi_w = w_hi[:, s, :, :].rearrange("p k n -> p (k n)")[:, 0:ks * n].rearrange("p (k n) -> p k n", n=n)
                lo_w = w_lo[:, s, :, :].rearrange("p k n -> p (k n)")[:, 0:ks * n].rearrange("p (k n) -> p k n", n=n)
                for t, b in enumerate(banks):
                    if first:
                        prior = ph.banks.index(b) + 1
                        if isinstance(i, int) and i == 0:
                            if t == 0:
                                pe.wait_ge(bank_free, ph.bank0[0])
                        else:
                            pe.wait_ge(bank_free, lin(ph.bank0, i) - len(ph.banks) + prior)
                    dst = PS[:, b, 0:n]
                    toks = slice((t % 2) * P, (t % 2 + 1) * P)
                    for k in range(ks):
                        kt = kt0 + (16 if t >= 2 else 0) + k
                        x_hi, x_lo = acts[0][:, kt, toks], acts[1][:, kt, toks]
                        begin, end = first and k == 0, final and k == ks - 1
                        nc.tensor.matmul(dst, x_hi, hi_w[:, k, :], start=begin, stop=False)
                        nc.tensor.matmul(dst, x_hi, lo_w[:, k, :], start=False, stop=False)
                        last = nc.tensor.matmul(dst, x_lo, hi_w[:, k, :], start=False, stop=end)
                    if final and t < len(banks) - 1:
                        last.then_inc(bank_done, 1)
                last.then_inc(pe_used, 1)

            act1, act2 = (act1_hi, act1_lo), (act2_hi, act2_lo)

            def plain(ph, i, p):
                chunk(ph, i, p, act1, ph.banks, p * CK_T, p == 0, p == ph.chunks - 1)

            pe.wait_ge(setup_in, SETUP * 16)
            pe.wait_ge(c_silu, 1)
            o = 0
            for r, n in enumerate((96, 80, 128, 32)):
                nc.tensor.transpose(PS[:, 4, o:o + n], rows[0:n, r, :], ident[0:n, 0:n])
                o += n
            nc.tensor.transpose(PS[:, 4, o:o + 32], c_rows[:, :], ident[0:32, 0:32]).then_inc(vec_T, 1)

            def mod_chunk(ph, i, p, b, q):
                pe.wait_ge(hi_ready, lin(col(ph.index, p), i) + 1)
                pe.wait_ge(lo_ready, lin(col(ph.index, p), i) + 1)
                if q == 0 and not (isinstance(b, int) and b == 0):
                    pe.wait_ge(m_red, b * 1)
                for k in range(CK_T):
                    cond = c4[:, q * CK_T + k, :]
                    nc.tensor.matmul(PS[:, 7, :], cond, w_hi[:, p % SPL, k, :], start=(q == 0 and k == 0), stop=False)
                    last = nc.tensor.matmul(PS[:, 7, :], cond, w_lo[:, p % SPL, k, :], start=False,
                                            stop=(q == 3 and k == CK_T - 1))
                last.then_inc(pe_used, 1)

            def mod_turn(b):
                pe.wait_ge(m_copied, b + 1)
                for j in range(4):
                    last = nc.tensor.transpose(PS[:, 7, j * P:(j + 1) * P], res4[:, j * P:(j + 1) * P], ident[:, :])
                last.then_inc(m_T, 1)

            pe.wait_ge(c_split, 2)

            def mod_block(i):
                for p in range(4):
                    if p == 0 and not (isinstance(i, int) and i == 0):
                        mod_turn(i - 1)
                    mod_chunk(p_mod, i, p, i, p)

            each_block(pe, p_mod.n, mod_block)
            mod_turn(p_mod.n - 1)

            def turn_x(stream, first, pair):
                transpose_groups(pe, first, lambda t, k: x_tok[:, 2 * stream + t, k * P:(k + 1) * P],
                                 range(2 * pair, 2 * pair + 2))

            def kv_block(i):
                for p in range(4):
                    if i == 0:
                        if p < 3:
                            both_streams(lambda w, first: turn_x(w, first, p + 1), p + 1)
                        pe.wait_ge(tp_lo, 4 * p + 4)
                    plain(p_kv, i, p)

            pe.wait_ge(n_mul, 4)
            both_streams(lambda w, first: turn_x(w, first, 0), 0)
            each_block(pe, p_kv.n, kv_block)
            for ph in (p_xb, p_dt):
                each_block(pe, ph.n, lambda i: [plain(ph, i, p) for p in range(ph.chunks)])

            pe.wait_ge(d_dve, D_A)
            pe.wait_ge(consts, 1)
            for ch in range(4):
                for d in range(2):
                    nc.tensor.matmul(PS[:, 7, ch * 64 + d * 32:ch * 64 + d * 32 + 32], tri[:, d, :],
                                     av[:, ch, d * 32:d * 32 + 32], start=True, stop=True)
            nc.tensor.matmul(PS[:, 7, 256:512], ones[:, :], av[:, :, :].rearrange("p a b -> p (a b)"),
                             start=True, stop=True).then_inc(d_pe, 1)

            for ph in (p_q, p_c):
                each_block(pe, ph.n, lambda i: [plain(ph, i, p) for p in range(ph.chunks)])

            def scores(i, u):
                h, t = u // 2, u % 2
                if not (isinstance(i, int) and i == 0 and u < 2):
                    pe.wait_ge(a_exp, i * 8 + (u - 1))
                nc.tensor.matmul(PS[:, 2 + u % 2, :], qT[:, h, t * P:(t + 1) * P], kT[:, :],
                                 start=True, stop=True).then_inc(a_sc, 1)

            def turn_probs(i, u):
                pe.wait_ge(a_norm, i * 8 + (u + 1))
                if not (isinstance(i, int) and i == 0 and u < 2):
                    pe.wait_ge(a_pTs, i * 8 + (u - 1))
                for k in range(4):
                    last = nc.tensor.transpose(PS[:, 4 + u % 2, k * P:(k + 1) * P], probs[:, u % 2, k * P:(k + 1) * P],
                                               ident[:, :])
                last.then_inc(a_pT, 1)

            def values(i, h):
                pe.wait_ge(a_pTs, i * 8 + (2 * h + 2))
                pe.wait_ge(a_vin, i * 32 + 32)
                if not (isinstance(i, int) and i == 0 and h == 0):
                    pe.wait_ge(a_o, i * REP + h)
                for k in range(4):
                    last = nc.tensor.matmul(PS[:, 6, 0:T], vv[:, k, :], pT[:, h % 2, k, :],
                                            start=(k == 0), stop=(k == 3))
                last.then_inc(a_pv, 1)

            def attention_start(i):
                pe.wait_ge(a_rope, i + 1)
                if not (isinstance(i, int) and i == 0):
                    pe.wait_ge(a_pTs, i * 8)
                    pe.wait_ge(a_o, i * REP)
                for h in range(REP):
                    for t in range(2):
                        nc.tensor.transpose(PS[:, 4 + h // 2, (h % 2) * T + t * P:(h % 2) * T + (t + 1) * P],
                                            qk_r[:, 5 * t + h, :], ident[:, :])
                for t in range(2):
                    nc.tensor.transpose(PS[:, 6, t * P:(t + 1) * P], qk[:, 10 + t, :], ident[:, :])
                    last = nc.tensor.transpose(PS[:, 6, (2 + t) * P:(3 + t) * P], qk_r[:, 5 * t + 4, :], ident[:, :])
                last.then_inc(a_qkT, 1)

            def attention_steps(i, lo, hi):
                for s in range(lo, hi):
                    if s >= 4 and s % 2 == 0:
                        values(i, (s - 4) // 2)
                    if 2 <= s <= 9:
                        turn_probs(i, s - 2)
                    if s < 8:
                        scores(i, s)

            pe.wait_ge(d_act, 6)
            pe.wait_ge(d_dve, D_END)

            def z_step(i):
                for p, what in enumerate(ORDER["z"]):
                    q = int(what[1])
                    if p == 2:
                        pe.wait_ge(a_qkS, i + 1)
                    if p >= 2:
                        attention_steps(i, p - 2, p - 1 if p < 11 else 11)
                    if what[0] == "m":
                        mod_chunk(p_z, i, p, i * 2 + (8 + q // 4), q % 4)
                    else:
                        chunk(p_z, i, p, act1, LAT, q * CK_T, q == 0, q == 3)
                    if p == 0 and not (isinstance(i, int) and i == 0):
                        mod_turn(i * 2 + 7)
                    if p == 6:
                        mod_turn(i * 2 + 8)
                    if p == 0:
                        attention_start(i)

            each_block(pe, p_z.n, z_step)

            def conv_in(g):
                pe.wait_ge(s_in, g * 80 + 80)
                if isinstance(g, int) and g == 0:
                    pe.wait_ge(a_o, AH)
                    pe.wait_ge(a_pTs, 8 * KVH)
                else:
                    pe.wait_ge(s_y2, g * 1)
                for m in range(7):
                    for t in range(2):
                        src = u_lat[:, t, m * P:(m + 1) * P] if m < 4 else u_ctx[:, t, (m - 4) * P:(m - 3) * P]
                        last = nc.tensor.transpose(PS[:, 2 + m // 2, (m % 2) * T + t * P:(m % 2) * T + (t + 1) * P],
                                                   src, ident[:, :])
                last.then_inc(s_Tin, 1)

            def back_to_rows(g):
                pe.wait_ge(s_D, g * 4 + 4)
                pe.wait_ge(s_silu, g + 1)
                for ch in range(4):
                    t = ch % 2
                    for j in range(3):
                        tile = j if ch >= 2 else 4 + j
                        last = nc.tensor.transpose(PS[:, 2 + ch, j * P:(j + 1) * P], cv[:, tile, t * P:(t + 1) * P],
                                                   ident[:, :])
                last.then_inc(s_Tb, 1)
                for c in range(2):
                    last = nc.tensor.matmul(PS[:, 6, c * P:(c + 1) * P], cv[:, 2, c * P:(c + 1) * P],
                                            cv[:, 3, c * P:(c + 1) * P], start=True, stop=True)
                last.then_inc(s_cb, 1)

            def decays(g):
                pe.wait_ge(s_cin, g + 1)
                pe.wait_ge(s_loc, g + 1)
                pe.wait_ge(s_neg, 1)
                for c in range(2):
                    for d in range(2):
                        bank = PS[:, 2 + 2 * c + d, :]
                        nc.tensor.matmul(bank, ident[:, :], negm[:, d, :].unsqueeze(1).to_broadcast([P, HPG, P]),
                                         start=True, stop=False, skip_group_check=True)
                        for h in range(HPG):
                            last = nc.tensor.matmul(bank[:, h * P:(h + 1) * P],
                                                    a_loc[:, c, d, h:h + 1].to_broadcast([P, P]), tri[:, d, :],
                                                    start=False, stop=True, skip_group_check=True)
                last.then_inc(s_dc, 1)

            def states(g):
                pe.wait_ge(s_tok, g + 1)
                pe.wait_ge(s_xw, g + 1)
                for d, xd in ((0, xdf), (1, xdb)):
                    for ch in range(2):
                        last = nc.tensor.matmul(PS[:, 3, d * 256:(d + 1) * 256], tokb[:, ch, 256:384], xd[:, ch, :],
                                                start=(ch == 0), stop=(ch == 1))
                last.then_inc(s_H, 1)
                nc.tensor.matmul(PS[:, 2, 0:256], tokb[:, 2, 256:384], xdf[:, 2, :], start=True, stop=True)
                nc.tensor.matmul(PS[:, 2, 256:512], tokb[:, 3, 256:384], xdb[:, 2, :],
                                 start=True, stop=True).then_inc(s_S, 1)

            def outputs(g):
                pe.wait_ge(s_h0, g + 1)
                pe.wait_ge(s_h1, g + 1)
                for c in range(2):
                    last = nc.tensor.matmul(PS[:, 4 + c, :], cv[:, 3, c * P:(c + 1) * P],
                                            hst[:, c, :, :].rearrange("p d n -> p (d n)"), start=True, stop=True)
                last.then_inc(s_yo, 1)
                pe.wait_ge(s_M, g + 1)
                for c in range(2):
                    for h in range(HPG):
                        for d in range(2):
                            last = nc.tensor.matmul(PS[:, 6, c * 256 + h * HD:c * 256 + (h + 1) * HD],
                                                    dec[:, 2 * c + d, h, :], xdt[:, d, c, h * HD:(h + 1) * HD],
                                                    start=(d == 0), stop=(d == 1))
                last.then_inc(s_yd, 1)

            def g_step(i):
                conv_in(i)
                for p, what in enumerate(ORDER["g"]):
                    q = int(what[1])
                    if p in (1, 4, 6, 7):
                        {1: decays, 4: back_to_rows, 6: states, 7: outputs}[p](i)
                    if what[0] == "m":
                        mod_chunk(p_g, i, p, i + 16, q)
                    else:
                        chunk(p_g, i, p, act1, LAT, q * CK_T, q == 0, q == 3)
                    if p == 0:
                        mod_turn(i + 15)

            each_block(pe, p_g.n, g_step)
            mod_turn(23)

            def gate_row(m):
                pe.wait_ge(dg_ready, m + 1)
                if not (isinstance(m, int) and m == 0):
                    pe.wait_ge(gt_ready, m * 1)
                nc.tensor.matmul(PS[:, 7, :], ones[:, :], diag[:, :, :].rearrange("p a b -> p (a b)"),
                                 start=True, stop=True).then_inc(dg_T, 1)

            def br_block(i):
                for p in range(8):
                    if isinstance(i, int) and i == 0 and p == 4:
                        pe.wait_ge(tp_lo, G_M)
                    chunk(p_br, i, p, act1, [0, 1] if p < 4 else [2, 3], (16 if p < 4 else 0) + (p % 4) * CK_T,
                          p % 4 == 0, p % 4 == 3)
                    if isinstance(i, int) and i == 0 and p < 4:
                        if p == 0:
                            pe.wait_ge(s_yz, GROUPS)
                            pe.wait_ge(y_in, 16)
                        transpose_groups(pe, G_Y, lambda t, k: wide[:, t, k * P:(k + 1) * P], range(2 * p, 2 * p + 2))
                    if p in (5, 7):
                        gate_row(i * 2 + (p - 5) // 2)

            each_block(pe, p_br.n, br_block)
            pe.wait_ge(g_ev, 4)

            def turn_ahead(first, i, p):
                if isinstance(i, int) and i == 0 and p < 4:
                    if p < 3:
                        transpose_groups(pe, first, lambda t, k: wide[:, t, k * P:(k + 1) * P], range(2 * p + 2, 2 * p + 4))
                    pe.wait_ge(tp_lo, first + 2 * p + 2)

            def o_block(i):
                for p in range(4):
                    turn_ahead(G_M, i, p)
                    plain(p_o, i, p)

            transpose_groups(pe, G_M, lambda t, k: wide[:, t, k * P:(k + 1) * P], range(2))
            each_block(pe, p_o.n, o_block)
            pe.wait_ge(n_mul, 6)
            transpose_groups(pe, G_H2, lambda t, k: wide[:, t, k * P:(k + 1) * P], range(2))

            def f1_chunk(i, p):
                chunk(p_f1, i, p, act2, [0, 1] if p < 4 else [2, 3], H2 + (p % 4) * CK_T, p % 4 == 0, p % 4 == 3)

            def turn_hidden(i):
                pe.wait_ge(bank_free, lin(p_f1.bank0, i) + 4)
                if not (isinstance(i, int) and i == 0):
                    pe.wait_ge(f_lo, i * 1)
                for k in range(4):
                    for t in range(2):
                        last = nc.tensor.transpose(PS[:, 4 + k // 2, (k % 2) * T + t * P:(k % 2) * T + (t + 1) * P],
                                                   stage[:, t, k * P:(k + 1) * P], ident[:, :])
                last.then_inc(f_T, 1)

            def f1_block(i):
                for p in range(8):
                    turn_ahead(G_H2, i, p)
                    f1_chunk(i, p)
                    if p == 1 and not (isinstance(i, int) and i == 0):
                        turn_hidden(i - 1)

            each_block(pe, p_f1.n, f1_block)
            turn_hidden(p_f1.n - 1)
            pe.wait_ge(f_lo, p_f1.n)
            each_block(pe, p_f2.n, lambda i: [chunk(p_f2, i, p, act2, LAT, p * CK_T, p == 0, p == p_f2.chunks - 1)
                                              for p in range(p_f2.chunks)])

        @block.scalar
        def _(act):
            small = [(ident[:, :], a["c_ident"]), (tri[:, 0, :], a["c_tri_f"]), (tri[:, 1, :], a["c_tri_b"]),
                     (rows[0:96, 0, :], a["b_mod"][0].rearrange("(r c) -> r c", c=P)),
                     (rows[0:16, 1, :], a["norm1"][0].rearrange("(r c) -> r c", c=P)),
                     (rows[16:32, 1, :], a["norm2"][0].rearrange("(r c) -> r c", c=P)),
                     (rows[32:48, 1, :], a["ssm_norm"][0].rearrange("(r c) -> r c", c=P)),
                     (rows[48:80, 1, :], a["conv_b"][0].rearrange("(r c) -> r c", c=P)),
                     (rows[:, 2, :], a["conv_w"][0].rearrange("j (r c) -> (j r) c", c=P)[0:P, :]),
                     (rows[0:32, 3, :], a["conv_w"][0].rearrange("j (r c) -> (j r) c", c=P)[P:P + 32, :]),
                     (c_rows[0:16, :], a["c"][0].rearrange("(r c) -> r c", c=P)),
                     (c_rows[16:32, :], a["c_ctx"].rearrange("(r c) -> r c", c=P)),
                     (dskip[:, :], a["d_skip"][0:1, :].to_broadcast([P, HEADS])),
                     (dtb[:, :], a["dt_bias"].rearrange("a d h -> a (d h)").to_broadcast([P, 64])),
                     (aneg[:, :], a["a_log"].rearrange("a d h -> a (d h)").to_broadcast([P, 64]))]
            assert len(small) == SETUP
            for dst, src in small:
                act.dma_start(dst, src).then_inc(setup_in, 16)
            act.wait_ge(setup_in, 16 * SETUP)
            nc.scalar.activation(c_rows[:, :], c_rows[:, :], ACT.Silu).then_inc(c_silu, 1)
            nc.scalar.activation(aneg[:, :], aneg[:, :], ACT.Exp).then_inc(c_silu, 1)

            def high(ph, i, p):
                act.wait_ge(raw_loaded[p % RAW], lin(col(ph.loaded, p), i))
                wait_split_slot(act, ph, i, p)
                dst, src = w_hi[:, p % SPL, :, :], raw[:, p % RAW, :, :]
                if ph is p_dt:
                    dst, src = [v.rearrange("p k n -> p (k n)")[:, 0:KT * 64] for v in (dst, src)]
                nc.scalar.activation(dst, src, ACT.Copy).then_inc(hi_ready, 1)

            def stage_out(ph, i):
                for b, bank in enumerate(ph.banks):
                    wait_bank(act, ph, i, b)
                    if not isinstance(i, int) or ph.stage0[i][b]:
                        act.wait_ge(stored[b], lin([s[b] for s in ph.stage0], i))
                    nc.scalar.activation(stage[:, b, :], PS[:, bank, :], ACT.Copy).then_inc(bank_free, 1)
                for b in range(len(ph.banks)):
                    act.wait_ge(bank_free, lin(ph.bank0, i) + b + 1)
                    dst = (proj_lat if b < 2 else proj_ctx)[(b % 2) * P:(b % 2 + 1) * P,
                                                            bass.ds(i * NB + PROJ_COL[ph.name], NB)]
                    act.dma_start(dst, stage[:, b, :]).then_inc(stored[b], 16)

            pending = [lambda: None]

            def stream(ph, evac, after=lambda i, p, last: None, loop=None):
                def body(i, last=None):
                    for p in range(ph.chunks):
                        high(ph, i, p)
                        if p == 0:
                            if isinstance(i, int) and i == 0:
                                pending[0]()
                            else:
                                evac(i - 1)
                        after(i, p, last)
                (loop or each_block)(act, ph.n, body)
                pending[0] = lambda: evac(ph.n - 1)

            def mod_out(chunks_done, b):
                act.wait_ge(pe_used, chunks_done)
                if not (isinstance(b, int) and b == 0):
                    act.wait_ge(m_T, b * 1)
                nc.scalar.activation(res4[:, :], PS[:, 7, :], ACT.Copy).then_inc(m_copied, 1)

            def mod_end(ph, i, p):
                return lin(col(ph.index, p), i) + 1

            def mod_after(i, p, last):
                if isinstance(i, int) and i == 0:
                    if p == 0:
                        act.wait_ge(x_loaded, 32)
                    else:
                        act.wait_ge(n_sq, p)
                    nc.scalar.activation(junk, x_tok[:, p, :], ACT.Square, accum_out=stat[:, p:p + 1]).then_inc(n_sq, 1)
                elif isinstance(i, int) and p == 0:
                    act.wait_ge(n_sq, 4)
                    act.wait_ge(consts, 2)
                    nc.scalar.activation(stat[:, 4:8], stat[:, 0:4], ACT.Sqrt, scale=1.0 / D,
                                         bias=stat[:, 15:16]).then_inc(n_sqrt, 1)

            stream(p_mod, lambda i: mod_out(mod_end(p_mod, i, 3), i), mod_after, two_peeled)
            pending[0]()
            pending[0] = lambda: None

            def x_high(pair):
                both_streams(lambda w, first: high_groups(act, first, act1_hi, 16 * w, range(2 * pair, 2 * pair + 2)), pair)

            x_high(0)
            stream(p_kv, lambda i: stage_out(p_kv, i), lambda i, p, last: x_high(p + 1) if i == 0 and p < 3 else None)
            stream(p_xb, lambda i: stage_out(p_xb, i))
            stream(p_dt, lambda i: None)
            act.wait_ge(bank_free, p_dt.banks_end)
            nc.scalar.activation(av[:, :, :], dt[:, :, :], ACT.Abs).then_inc(d_act, 1)
            act.wait_ge(d_act, 1)
            nc.scalar.activation(av[:, :, :], av[:, :, :], ACT.Exp, scale=-1.0).then_inc(d_act, 1)
            act.wait_ge(d_dve, 1)
            nc.scalar.activation(etot[:, :, :], acum[:, :, :], ACT.Ln).then_inc(d_act, 1)
            act.wait_ge(d_dve, D_A + 2)
            nc.scalar.activation(etot[:, :, :].rearrange("p a b -> p (a b)"), PS[:, 7, 256:512],
                                 ACT.Exp).then_inc(d_act, 1)
            nc.scalar.activation(eacum[:, :, :].rearrange("p a b -> p (a b)"), PS[:, 7, 0:256],
                                 ACT.Exp).then_inc(d_act, 1)
            nc.scalar.activation(wdec[:, :, :], wdec[:, :, :], ACT.Exp).then_inc(d_act, 1)

            stream(p_q, lambda i: stage_out(p_q, i))

            def rms_root(i):
                act.wait_ge(a_ssq, i + 1)
                nc.scalar.activation(ast[:, 12:24], ast[:, 0:12], ACT.Sqrt, scale=1.0 / AD,
                                     bias=stat[:, 15:16]).then_inc(a_sqrt, 1)

            def attention_start(i):
                act.wait_ge(a_qkT, i + 1)
                if not (isinstance(i, int) and i == 0):
                    act.wait_ge(a_sc, i * 8)
                nc.scalar.activation(qT[:, :, :].rearrange("p (b h) t -> p b (h t)", b=2), PS[:, 4:6, :], ACT.Copy)
                nc.scalar.activation(kT[:, :], PS[:, 6, :], ACT.Copy).then_inc(a_qkS, 1)

            def attention_steps(i, lo, hi):
                for s in range(lo, hi):
                    if 2 <= s <= 9:
                        u = s - 2
                        h, t = u // 2, u % 2
                        act.wait_ge(a_pT, i * 8 + (u + 1))
                        if not (isinstance(i, int) and i == 0 and h < 2):
                            act.wait_ge(a_pv, i * REP + (h - 1))
                        nc.scalar.activation(pT[:, h % 2, :, t * P:(t + 1) * P],
                                             PS[:, 4 + u % 2, :].rearrange("p (k q) -> p k q", k=4),
                                             ACT.Copy).then_inc(a_pTs, 1)
                    if s < 8:
                        act.wait_ge(a_max, i * 8 + (s + 1))
                        if not (isinstance(i, int) and i == 0 and s < 2):
                            act.wait_ge(a_pT, i * 8 + (s - 1))
                        nc.scalar.activation(probs[:, s % 2, :], PS[:, 2 + s % 2, :], ACT.Exp,
                                             bias=ast[:, 36 + s % 2:37 + s % 2],
                                             accum_out=ast[:, 40 + s % 2:41 + s % 2]).then_inc(a_exp, 1)
                    if s >= 4 and s % 2 == 0:
                        h = (s - 4) // 2
                        act.wait_ge(a_pv, i * REP + (h + 1))
                        nc.scalar.activation(act1_hi[:, bass.ds(i * REP + (16 + h), 1), :], PS[:, 6, 0:T],
                                             ACT.Copy).then_inc(a_ohi, 1)

            def z_after(i, p, last):
                if p == 0:
                    if not (isinstance(i, int) and i == 0):
                        mod_out(mod_end(p_z, i - 1, 11), i * 2 + 7)
                if p == 1:
                    attention_start(i)
                if p == 6:
                    mod_out(mod_end(p_z, i, 5), i * 2 + 8)
                if p >= 2:
                    attention_steps(i, p - 2, p - 1 if p < 11 else 11)
                if p == 6 and not last:
                    rms_root(i + 1)

            def c_after(i, p, last):
                if i == 1 and p == 2:
                    rms_root(0)

            stream(p_c, lambda i: stage_out(p_c, i), c_after)
            stream(p_z, lambda i: stage_out(p_z, i), z_after, pipelined)

            def y_root(g):
                act.wait_ge(s_yz, g + 1)
                for c in range(2):
                    last = nc.scalar.activation(yt[:, c, 0:256], yb[:, c, :], ACT.Square,
                                                accum_out=sst[:, c:c + 1])
                last.then_inc(s_sqa, 1)
                act.wait_ge(s_sqa, g + 1)
                nc.scalar.activation(sst[:, 2:4], sst[:, 0:2], ACT.Sqrt, scale=1.0 / 256,
                                     bias=stat[:, 15:16]).then_inc(s_sq, 1)

            def store_y(g):
                act.wait_ge(s_y, g + 1)
                act.dma_start(rows2(y_dram, g * 256, 256), yb[:, :, :]).then_inc(s_yst, 16)

            def g_after(g, p, last):
                if p == 2 and not (isinstance(g, int) and g == 0):
                    store_y(g - 1)
                if p == 0:
                    mod_out(mod_end(p_z, p_z.n - 1, 11) if isinstance(g, int) and g == 0 else
                            mod_end(p_g, g - 1, 7), g + 15)
                    act.wait_ge(s_Tin, g + 1)
                    if isinstance(g, int) and g == 0:
                        act.wait_ge(s_pre, 1)
                    for q in range(4):
                        m = 2 if q < 3 else 1
                        last = nc.scalar.activation(cin[:, 2 * q:2 * q + m, 2:T + 2],
                                                    PS[:, 2 + q, 0:m * T].rearrange("p (m t) -> p m t", t=T), ACT.Copy)
                    last.then_inc(s_cin, 1)
                    if not (isinstance(g, int) and g == 0):
                        y_root(g - 1)
                if p == 2:
                    act.wait_ge(s_tap, g * TAPS + TAPS)
                    for m in range(7):
                        tile = g * 2 + (48 + m % 4) if m % 4 < 2 else g + (48 + 16 if m % 4 == 2 else 48 + 24)
                        last = nc.scalar.activation(cv[:, m, :], cv[:, m, :], ACT.Silu, bias=vec_col[:, bass.ds(tile, 1)])
                    last.then_inc(s_silu, 1)
                    act.wait_ge(s_zin, g * 16 + 16)
                    nc.scalar.activation(zt[:, :, :], zt[:, :, :], ACT.Silu).then_inc(s_zs, 1)
                if p == 3:
                    act.wait_ge(s_D, g * 4 + 4)
                    nc.scalar.activation(dec[:, :, :, :], dec[:, :, :, :], ACT.Exp).then_inc(s_E, 1)
                if p == 4:
                    act.wait_ge(s_Tb, g + 1)
                    for ch in range(4):
                        last = nc.scalar.activation(tokb[:, ch, :], PS[:, 2 + ch, 0:384], ACT.Copy)
                    last.then_inc(s_tok, 1)
                if p == 6:
                    act.wait_ge(s_H, g + 1)
                    nc.scalar.activation(hst[:, 0, 0, :], PS[:, 3, 0:256], ACT.Copy)
                    nc.scalar.activation(hst[:, 1, 1, :], PS[:, 3, 256:512], ACT.Copy).then_inc(s_h0, 1)

            stream(p_g, lambda i: stage_out(p_g, i), g_after)
            y_root(GROUPS - 1)
            store_y(GROUPS - 1)
            pending[0]()
            mod_out(mod_end(p_g, p_g.n - 1, 7), 23)

            def br_after(i, p, last):
                if isinstance(i, int) and i == 0 and 1 <= p <= 4:
                    high_groups(act, G_Y, act1_hi, 0, range(2 * p - 2, 2 * p))
                if p == 4:
                    act.wait_ge(g_in, i * 32 + 32)
                    nc.scalar.activation(gates[:, :, :, :], gates[:, :, :, :], ACT.Sigmoid).then_inc(g_sig, 1)
                if p == 7:
                    act.wait_ge(dg_T, i * 2 + 1)
                    nc.scalar.activation(gt1[:, bass.ts(i, NB)], PS[:, 7, :], ACT.Copy).then_inc(gt_ready, 1)
                if p == 0 and not (isinstance(i, int) and i == 0):
                    gate2_row(i - 1)

            def gate2_row(i):
                act.wait_ge(dg_T, i * 2 + 2)
                if not (isinstance(i, int) and i == 0):
                    act.wait_ge(g2_out, i * 16)
                nc.scalar.activation(g2t[:, :], PS[:, 7, :], ACT.Copy).then_inc(gt_ready, 1)
                act.wait_ge(gt_ready, i * 2 + 2)
                act.dma_start(gate2_dram[:, bass.ts(i, NB)], g2t[0:1, :]).then_inc(g2_out, 16)

            pending[0] = lambda: None
            stream(p_br, lambda i: None, br_after)
            gate2_row(p_br.n - 1)

            def high_ahead(first, hi, k0, i, p):
                if isinstance(i, int) and i == 0 and p < 3:
                    high_groups(act, first, hi, k0, range(2 * p + 2, 2 * p + 4))

            high_groups(act, G_M, act1_hi, 0, range(2))
            stream(p_o, lambda i: None, lambda i, p, last: high_ahead(G_M, act1_hi, 0, i, p))
            act.wait_ge(o_ev, 4)
            for t in range(2):
                if t > 0:
                    act.wait_ge(n_sq, 4 + t)
                nc.scalar.activation(junk, xres[:, t, :], ACT.Square, accum_out=stat[:, 8 + t:9 + t]).then_inc(n_sq, 1)
            act.wait_ge(n_sq, 6)
            nc.scalar.activation(stat[:, 10:12], stat[:, 8:10], ACT.Sqrt, scale=1.0 / D,
                                 bias=stat[:, 15:16]).then_inc(n_sqrt, 1)
            act.wait_ge(pe_used, p_o.index[-1][-1] + 1)
            high_groups(act, G_H2, act2_hi, H2, range(2))

            def gate_out(i):
                for t in range(2):
                    wait_bank(act, p_f1, i, t)
                    if not (isinstance(i, int) and i == 0):
                        act.wait_ge(f_T, i * 1)
                    nc.scalar.activation(stage[:, t, :], PS[:, t, :], ACT.Silu).then_inc(bank_free, 1)

            def hidden_high(i):
                act.wait_ge(f_T, i + 1)
                nc.scalar.activation(act2_hi[:, bass.ds(i * 4, 4), :].rearrange("p (b k) t -> p b (k t)", b=2),
                                     PS[:, 4:6, :], ACT.Copy).then_inc(f_hi, 1)

            def f1_after(i, p, last):
                high_ahead(G_H2, act2_hi, H2, i, p)
                if p == 2 and not (isinstance(i, int) and i == 0):
                    hidden_high(i - 1)

            stream(p_f1, gate_out, f1_after)
            pending[0] = lambda: (gate_out(p_f1.n - 1), hidden_high(p_f1.n - 1))
            def store_out(i):
                act.wait_ge(f2_ev, i + 1)
                act.dma_start(rows2(out[0], i * NB, NB), stage[:, 2:4, :]).then_inc(f2_out, 16)

            stream(p_f2, lambda i: None,
                   lambda i, p, last: store_out(i - 1) if p == 2 and not (isinstance(i, int) and i == 0) else None)
            store_out(p_f2.n - 1)
            act.wait_ge(f2_out, 16 * p_f2.n)

        @block.vector
        def _(dve):
            nc.vector.memset(ones[:, :], 1.0).then_inc(consts, 1)
            nc.vector.memset(stat[:, 15:16], EPS).then_inc(consts, 1)
            dve.wait_ge(c_silu, 2)
            nc.vector.tensor_scalar(aneg[:, :], aneg[:, :], -1.0, None, ALU.mult).then_inc(cols_ready, 1)
            dve.wait_ge(vec_T, 1)
            nc.vector.tensor_copy(b_col[:, :], PS[:, 4, 0:96]).then_inc(cols_ready, 1)
            nc.vector.tensor_copy(vec_col[:, :], PS[:, 4, 96:176]).then_inc(cols_ready, 1)
            nc.vector.tensor_copy(conv_w[:, :], PS[:, 4, 176:336]).then_inc(cols_ready, 1)
            nc.vector.tensor_copy(c_col[:, :], PS[:, 4, 336:368]).then_inc(cols_ready, 1)

            dve.wait_ge(cols_ready, 5)
            cond = c_col[:, :].rearrange("p (w k) -> p k w", w=2).unsqueeze(2).to_broadcast([P, KT, P // 4, 2])
            c4v = c4[:, :, :].rearrange("p k (r w l) -> p k r w l", w=2, l=2)
            nc.vector.tensor_copy(c4v[:, :, :, :, 0], cond).then_inc(c_split, 1)
            dve.wait_ge(c_split, 1)
            nc.vector.tensor_tensor(c4v[:, :, :, :, 1], cond, c4v[:, :, :, :, 0].bitcast(F32),
                                    ALU.subtract).then_inc(c_split, 1)

            def low(ph, i, p):
                dve.wait_ge(hi_ready, lin(col(ph.index, p), i) + 1)
                r, h, o = raw[:, p % RAW, :, :], w_hi[:, p % SPL, :, :].bitcast(F32), w_lo[:, p % SPL, :, :]
                if ph is p_dt:
                    r, h, o = [v.rearrange("p k n -> p (k n)")[:, 0:KT * 64] for v in (r, h, o)]
                nc.vector.tensor_tensor(o, r, h, ALU.subtract).then_inc(lo_ready, 1)

            pending = [lambda: None]

            def stream(ph, evac, after=lambda i, p, last: None, loop=None):
                def body(i, last=None):
                    for p in range(ph.chunks):
                        low(ph, i, p)
                        if p == 0:
                            if isinstance(i, int) and i == 0:
                                pending[0]()
                            else:
                                evac(i - 1)
                        after(i, p, last)
                (loop or each_block)(dve, ph.n, body)
                pending[0] = lambda: evac(ph.n - 1)

            nothing = lambda i: None

            def mod_cols(b):
                dve.wait_ge(m_T, b + 1)
                if not (isinstance(b, int) and b == 0):
                    dve.wait_ge(mod_ready, b * 1)
                turned = PS[:, 7, :].rearrange("p (j c) -> p j c", j=4)[:, :, 0:4].rearrange("p j (w l) -> p j w l", l=2)
                nc.vector.tensor_reduce(m2[:, :].rearrange("p (j w) -> p j w", w=2), turned, AX_X,
                                        ALU.add).then_inc(m_red, 1)
                dve.wait_ge(m_red, b + 1)
                nc.vector.tensor_tensor(mod[:, bass.ds(b * 4, 4), :], m2[:, :].rearrange("p (j w) -> p j w", w=2),
                                        b_col[:, bass.ds(b * 4, 4)].unsqueeze(2).to_broadcast([P, 4, 2]),
                                        ALU.add).then_inc(mod_ready, 1)

            def mod_after(i, p, last):
                if isinstance(i, int) and i == 1:
                    if p == 0:
                        dve.wait_ge(n_sqrt, 1)
                        nc.vector.reciprocal(stat[:, 4:8], stat[:, 4:8]).then_inc(n_rec, 1)
                        dve.wait_ge(n_rec, 1)
                    nc.vector.tensor_scalar(x_tok[:, p, :], x_tok[:, p, :], stat[:, 4 + p:5 + p], None,
                                            ALU.mult).then_inc(n_mul, 1)

            stream(p_mod, mod_cols, mod_after, two_peeled)
            pending[0]()
            pending[0] = lambda: None
            dve.wait_ge(mod_ready, 8)
            nc.vector.scalar_tensor_tensor(out=s1[:, :, :], in0=mod[:, 16:32, :], scalar=1.0,
                                           in1=vec_col[:, 0:16].unsqueeze(2).to_broadcast([P, KT, 2]),
                                           op0=ALU.add, op1=ALU.mult).then_inc(s1_ready, 1)
            dve.wait_ge(s1_ready, 1)

            def x_low(pair):
                both_streams(lambda w, first: low_groups(dve, first, act1_hi, act1_lo, 16 * w, lambda k: s1[:, k, w:w + 1],
                                                         lambda k: mod[:, k, w:w + 1], range(2 * pair, 2 * pair + 2)), pair)

            x_low(0)
            stream(p_kv, nothing, lambda i, p, last: x_low(p + 1) if i == 0 and p < 3 else None)
            stream(p_xb, nothing)
            stream(p_dt, nothing)

            k = [0]

            def step(ins, wait=True):
                k[0] += 1
                ins.then_inc(d_dve, 1)
                if wait:
                    dve.wait_ge(d_dve, k[0])

            dve.wait_ge(n_mul, 4)
            dve.wait_ge(tp_done, G_Y)
            for b in range(4):
                wait_bank(dve, p_dt, 0, b)
                ch = 2 + b if b < 2 else b - 2
                nc.vector.tensor_tensor(dt[:, ch, :], PS[:, b, 0:64], dtb[:, :], ALU.add).then_inc(bank_free, 1)
            dve.wait_ge(d_act, 2)
            step(nc.vector.tensor_scalar(acum[:, :, :], av[:, :, :], 1.0, None, ALU.add))
            step(nc.vector.tensor_scalar(eacum[:, :, :], acum[:, :, :], -1.0, None, ALU.add))
            step(nc.vector.tensor_tensor(eacum[:, :, :], av[:, :, :], eacum[:, :, :], ALU.subtract))
            step(nc.vector.reciprocal(wdec[:, :, :], acum[:, :, :]))
            step(nc.vector.tensor_tensor(eacum[:, :, :], eacum[:, :, :], wdec[:, :, :], ALU.mult))
            dve.wait_ge(d_act, 3)
            step(nc.vector.scalar_tensor_tensor(out=dt[:, :, :], in0=dt[:, :, :], scalar=0.0, in1=etot[:, :, :],
                                                op0=ALU.max, op1=ALU.add))
            step(nc.vector.tensor_tensor(dt[:, :, :], dt[:, :, :], eacum[:, :, :], ALU.add))
            step(nc.vector.tensor_tensor(av[:, :, :], dt[:, :, :],
                                         aneg[:, :].unsqueeze(1).to_broadcast([P, 4, 64]), ALU.mult))
            assert k[0] == D_A
            dve.wait_ge(d_pe, 1)
            step(nc.vector.tensor_copy(acum[:, :, :].rearrange("p a b -> p (a b)"), PS[:, 7, 0:256]))
            step(nc.vector.tensor_tensor(wdec[:, :, :].rearrange("p a b -> p (a b)"), PS[:, 7, 256:512],
                                         acum[:, :, :].rearrange("p a b -> p (a b)"), ALU.subtract))
            dve.wait_ge(d_act, 6)
            step(nc.vector.tensor_tensor(wdec[:, :, :], wdec[:, :, :], dt[:, :, :], ALU.mult))
            step(nc.vector.tensor_tensor(wdec[:, 0, 0:32], wdec[:, 0, 0:32], etot[:, 1, 0:32], ALU.mult))
            step(nc.vector.tensor_tensor(wdec[:, 1, 32:64], wdec[:, 1, 32:64], etot[:, 0, 32:64], ALU.mult))
            assert k[0] == D_END
            pending[0] = lambda: None
            stream(p_q, nothing)

            def rope_tables():
                dve.wait_ge(r_in, 16 * 8)
                nc.vector.tensor_scalar(gain5[:, 0:4, :], gain5[:, 0:4, :], float(AD) ** -0.5, None,
                                        ALU.mult).then_inc(r_dve, 1)
                dve.wait_ge(r_dve, 1)
                for t in range(2):
                    nc.vector.tensor_tensor(cos5[:, t, :, :], gain5[:, :, :],
                                            rope[:, t, 0, :].unsqueeze(1).to_broadcast([P, 5, AD]), ALU.mult)
                    g = gain5[:, :, :].rearrange("p h (a b f) -> p h a b f", a=2, b=2)
                    s = rope[:, t, 1, :].rearrange("p (a b f) -> p a b f", a=2, b=2)
                    o = sin5[:, t, :, :].rearrange("p h (a b f) -> p h a b f", a=2, b=2)
                    for b in range(2):
                        last = nc.vector.tensor_tensor(o[:, :, :, b, :], g[:, :, :, 1 - b, :],
                                                       s[:, :, b, :].unsqueeze(1).to_broadcast([P, 5, 2, 32]), ALU.mult)
                last.then_inc(r_dve, 1)
                dve.wait_ge(r_dve, 2)

            def prepare_1(i):
                dve.wait_ge(a_in, i * 80 + 80)
                if not (isinstance(i, int) and i == 0):
                    dve.wait_ge(a_qkT, i * 1)
                    dve.wait_ge(a_rope, i * 1)
                n = i * 4
                nc.vector.tensor_tensor(qk_sq[:, :, :], qk[:, :, :], qk[:, :, :], ALU.mult).then_inc(a_dve, 1)
                dve.wait_ge(a_dve, n + 1)
                nc.vector.tensor_reduce(ast[:, 0:12], qk_sq[:, :, :], AX_X, ALU.add).then_inc(a_ssq, 1)

            def prepare_2(i):
                n = i * 4
                dve.wait_ge(a_sqrt, i + 1)
                nc.vector.reciprocal(ast[:, 24:36], ast[:, 12:24]).then_inc(a_dve, 1)
                dve.wait_ge(a_dve, n + 2)
                nc.vector.tensor_tensor(qk[:, :, :], qk[:, :, :], ast[:, 24:36].unsqueeze(2).to_broadcast([P, 12, AD]),
                                        ALU.mult).then_inc(a_dve, 1)

            def prepare_3(i):
                dve.wait_ge(a_dve, i * 4 + 3)

                def halves(v):
                    return v.rearrange("p h (a b f) -> p (h a) b f", a=2, b=2)
                src, swp = halves(qk[:, 0:10, :]), halves(qk_sq[:, 0:10, :])
                sn = sin5[:, :, :, :].rearrange("p t h (a b f) -> p (t h a) b f", a=2, b=2)
                nc.vector.tensor_tensor(swp[:, :, 0, :], src[:, :, 1, :], sn[:, :, 0, :], ALU.mult)
                nc.vector.tensor_tensor(swp[:, :, 1, :], src[:, :, 0, :], sn[:, :, 1, :], ALU.mult)

            def prepare_4(i):
                n = i * 4
                nc.vector.tensor_tensor(qk_r[:, :, :], qk[:, 0:10, :],
                                        cos5[:, :, :, :].rearrange("p t h d -> p (t h) d"), ALU.mult)
                nc.vector.tensor_tensor(qk[:, 10:12, :], qk[:, 10:12, :],
                                        gain_k[:, :].unsqueeze(1).to_broadcast([P, 2, AD]), ALU.mult).then_inc(a_dve, 1)
                dve.wait_ge(a_dve, n + 4)
                nc.vector.tensor_tensor(qk_r[:, :, :], qk_r[:, :, :], qk_sq[:, 0:10, :], ALU.add).then_inc(a_rope, 1)

            def attention_steps(i, lo, hi):
                for s in range(lo, hi):
                    if 1 <= s <= 8:
                        u = s - 1
                        dve.wait_ge(a_exp, i * 8 + (u + 1))
                        nc.vector.reciprocal(ast[:, 44 + u % 2:45 + u % 2], ast[:, 40 + u % 2:41 + u % 2]).then_inc(a_rec, 1)
                        dve.wait_ge(a_rec, i * 8 + (u + 1))
                        nc.vector.tensor_scalar(probs[:, u % 2, :], probs[:, u % 2, :], ast[:, 44 + u % 2:45 + u % 2],
                                                None, ALU.mult).then_inc(a_norm, 1)
                    if s < 8:
                        dve.wait_ge(a_sc, i * 8 + (s + 1))
                        if not (isinstance(i, int) and i == 0 and s < 2):
                            dve.wait_ge(a_exp, i * 8 + (s - 1))
                        nc.vector.tensor_reduce(ast[:, 36 + s % 2:37 + s % 2], PS[:, 2 + s % 2, :], AX_X, ALU.max,
                                                negate=True).then_inc(a_max, 1)
                    if s >= 4 and s % 2 == 0:
                        h = (s - 4) // 2
                        dve.wait_ge(a_ohi, i * REP + (h + 1))
                        nc.vector.tensor_tensor(act1_lo[:, bass.ds(i * REP + (16 + h), 1), :],
                                                PS[:, 6, 0:T].unsqueeze(1),
                                                act1_hi[:, bass.ds(i * REP + (16 + h), 1), :].bitcast(F32),
                                                ALU.subtract).then_inc(a_o, 1)

            def z_after(i, p, last):
                if p == 1 and not (isinstance(i, int) and i == 0):
                    mod_cols(i * 2 + 7)
                if p == 7:
                    mod_cols(i * 2 + 8)
                if p >= 2:
                    attention_steps(i, p - 2, p - 1 if p < 11 else 11)
                if p in (5, 8, 9, 10) and not last:
                    {5: prepare_1, 8: prepare_2, 9: prepare_3, 10: prepare_4}[p](i + 1)

            def c_after(i, p, last):
                if i == 1 and p == 1:
                    rope_tables()
                    prepare_1(0)
                if i == 1 and p == 2:
                    prepare_2(0)
                    prepare_3(0)
                    prepare_4(0)

            stream(p_c, nothing, c_after)
            stream(p_z, nothing, z_after, pipelined)

            def heads(v, d, g):
                return v[..., bass.ds(g * HPG + d * 32, HPG)]

            def y_scale(g):
                dve.wait_ge(s_sq, g + 1)
                nc.vector.reciprocal(sst[:, 4:6], sst[:, 2:4]).then_inc(s_rec, 1)
                dve.wait_ge(s_rec, g + 1)
                dve.wait_ge(s_yz, g + 1)
                for c in range(2):
                    ins = nc.vector.tensor_scalar(yb[:, c, :], yb[:, c, :], sst[:, 4 + c:5 + c], None, ALU.mult)
                ins.then_inc(s_y, 1)

            def g_after(g, p, last):
                if p == 1:
                    mod_cols(g + 15)
                    if not (isinstance(g, int) and g == 0):
                        y_scale(g - 1)
                if p == 0:
                    if isinstance(g, int) and g == 0:
                        dve.wait_ge(a_pv, AH)
                        dve.wait_ge(a_ohi, AH)
                        nc.vector.tensor_scalar(negm[:, :, :], tri[:, :, :], -1.0, 1e30, ALU.add,
                                                ALU.mult).then_inc(s_neg, 1)
                    for d in range(2):
                        ins = nc.vector.tensor_copy(a_loc[:, :, d, :], heads(av[:, 2:4, :], d, g))
                    ins.then_inc(s_loc, 1)
                    dve.wait_ge(s_cin, g + 1)
                if p <= 2:
                    for tap in ((0, 1), (2, 3), (4,))[p]:
                        if tap:
                            dve.wait_ge(s_tap, g * TAPS + tap)
                        for m in range(7):
                            tile = g * 2 + (32 * tap + m % 4) if m % 4 < 2 else g + (32 * tap + (16 if m % 4 == 2 else 24))
                            w = conv_w[:, bass.ds(tile, 1)]
                            src = cin[:, m, tap:tap + T]
                            if tap == 0:
                                ins = nc.vector.tensor_scalar(cv[:, m, :], src, w, None, ALU.mult)
                            else:
                                ins = nc.vector.scalar_tensor_tensor(out=cv[:, m, :], in0=src, scalar=w, in1=cv[:, m, :],
                                                                     op0=ALU.mult, op1=ALU.add)
                        ins.then_inc(s_tap, 1)
                if p == 2:
                    dve.wait_ge(s_dc, g + 1)
                    for c in range(2):
                        for d in range(2):
                            nc.vector.tensor_tensor(
                                dec[:, 2 * c + d, :, :], PS[:, 2 + 2 * c + d, :].rearrange("p (h l) -> p h l", h=HPG),
                                heads(acum[:, 2 + c, :], d, g).unsqueeze(2).to_broadcast([P, HPG, P]),
                                ALU.subtract).then_inc(s_D, 1)
                if p == 4:
                    dve.wait_ge(s_E, g + 1)
                    dve.wait_ge(s_cb, g + 1)
                    for c in range(2):
                        v = dec[:, 2 * c:2 * c + 2, :, :].rearrange("p d h l -> p (d h) l")
                        ins = nc.vector.tensor_tensor(
                            v, v, PS[:, 6, c * P:(c + 1) * P].unsqueeze(1).to_broadcast([P, 2 * HPG, P]), ALU.mult)
                    ins.then_inc(s_M, 1)
                if p == 5:
                    dve.wait_ge(s_tok, g + 1)
                    x_l = tokb[:, 2:4, 0:256].rearrange("p c (h n) -> p c h n", h=HPG)

                    def weigh(o, x, w, n):
                        return nc.vector.tensor_tensor(o.rearrange("p c (h n) -> p c h n", h=HPG), x,
                                                       w.unsqueeze(3).to_broadcast([P, n, HPG, HD]), ALU.mult)
                    for d in range(2):
                        weigh(xdt[:, d, :, :], x_l, heads(dt[:, 2:4, :], d, g), 2)
                    x_f = tokb[:, 0:3, 0:256].rearrange("p c (h n) -> p c h n", h=HPG)
                    weigh(xdf, x_f, heads(wdec[:, 0:3, :], 0, g), 3)
                    weigh(xdb[:, 0:2, :], x_f[:, 0:2, :, :], heads(wdec[:, 0:2, :], 1, g), 2)
                    weigh(xdb[:, 2:3, :], x_l[:, 1:2, :, :], heads(wdec[:, 3:4, :], 1, g), 1).then_inc(s_xw, 1)
                if p == 6:
                    dve.wait_ge(s_h0, g + 1)
                    for o, src, ch, d in ((hst[:, 1, 0, :], hst[:, 0, 0, :], 2, 0), (hst[:, 0, 1, :], hst[:, 1, 1, :], 3, 1)):
                        ins = nc.vector.tensor_tensor(o.rearrange("p (h n) -> p h n", h=HPG),
                                                      src.rearrange("p (h n) -> p h n", h=HPG),
                                                      heads(etot[:, ch, :], d, g).unsqueeze(2).to_broadcast([P, HPG, HD]),
                                                      ALU.mult)
                    ins.then_inc(s_ht, 1)
                    dve.wait_ge(s_ht, g + 1)
                    dve.wait_ge(s_S, g + 1)
                    nc.vector.tensor_tensor(hst[:, 1, 0, :], hst[:, 1, 0, :], PS[:, 2, 0:256], ALU.add)
                    nc.vector.tensor_tensor(hst[:, 0, 1, :], hst[:, 0, 1, :], PS[:, 2, 256:512], ALU.add).then_inc(s_h1, 1)
                if p == 7:
                    dve.wait_ge(s_yo, g + 1)
                    dve.wait_ge(s_yd, g + 1)
                    for c in range(2):
                        w = eacum[:, 2 + c, :].rearrange("p (d h) -> p d h", d=2)[:, :, bass.ds(g * HPG, HPG)]
                        nc.vector.tensor_tensor(yt[:, c, :].rearrange("p (d h n) -> p d h n", d=2, h=HPG),
                                                PS[:, 4 + c, :].rearrange("p (d h n) -> p d h n", d=2, h=HPG),
                                                w.unsqueeze(3).to_broadcast([P, 2, HPG, HD]), ALU.mult)
                    nc.vector.tensor_tensor(yx.rearrange("p c (h n) -> p c h n", h=HPG),
                                            tokb[:, 2:4, 0:256].rearrange("p c (h n) -> p c h n", h=HPG),
                                            dskip[:, bass.ds(g * HPG, HPG)].unsqueeze(1).unsqueeze(3)
                                            .to_broadcast([P, 2, HPG, HD]), ALU.mult).then_inc(s_y1, 1)
                    dve.wait_ge(s_y1, g + 1)
                    if not (isinstance(g, int) and g == 0):
                        dve.wait_ge(s_yst, g * 16)
                    nc.vector.tensor_tensor(yb[:, :, :], yt[:, :, 0:256], yt[:, :, 256:512], ALU.add)
                    nc.vector.tensor_tensor(yx, yx, PS[:, 6, :].rearrange("p (c n) -> p c n", c=2),
                                            ALU.add).then_inc(s_y2, 1)
                    dve.wait_ge(s_y2, g + 1)
                    nc.vector.tensor_tensor(yb[:, :, :], yb[:, :, :], yx, ALU.add).then_inc(s_y3, 1)
                    dve.wait_ge(s_y3, g + 1)
                    dve.wait_ge(s_zs, g + 1)
                    nc.vector.tensor_tensor(yb[:, :, :], yb[:, :, :], zt[:, :, :], ALU.mult).then_inc(s_yz, 1)

            stream(p_g, nothing, g_after)
            y_scale(GROUPS - 1)
            mod_cols(23)
            dve.wait_ge(mod_ready, 24)
            nc.vector.scalar_tensor_tensor(out=s2[:, :], in0=mod[:, 64:80, 0], scalar=1.0, in1=vec_col[:, 16:32],
                                           op0=ALU.add, op1=ALU.mult).then_inc(s2_ready, 1)

            def merge(i):
                dve.wait_ge(g_sig, i + 1)
                if not (isinstance(i, int) and i == 0):
                    dve.wait_ge(g_ev, i * 1)
                for b in range(4):
                    wait_bank(dve, p_br, i, b)
                    t, br = b % 2, b // 2
                    dst = wide[:, t, bass.ts(i, NB)] if br == 0 else tmp[:, t, :, :].rearrange("p a b -> p (a b)")
                    nc.vector.tensor_tensor(dst, PS[:, b, :], gates[:, br, t, :], ALU.mult).then_inc(bank_free, 1)
                dve.wait_ge(bank_free, lin(p_br.bank0, i) + 4)
                ins = nc.vector.tensor_tensor(wide[:, :, bass.ts(i, NB)], wide[:, :, bass.ts(i, NB)],
                                              tmp[:, :, :, :].rearrange("p t a b -> p t (a b)"), ALU.add)
                ins.then_inc(g_ev, 1)

            def diagonal(m, c0):
                if not (isinstance(m, int) and m == 0):
                    dve.wait_ge(dg_T, m * 1)
                for j in range(4):
                    ins = nc.vector.tensor_scalar(diag[:, j, :], ident[:, :], mod[:, bass.ds(c0 + j, 1), 0:1].rearrange(
                        "p a b -> p (a b)"), None, ALU.mult)
                ins.then_inc(dg_ready, 1)

            def br_after(i, p, last):
                if isinstance(i, int) and i == 0 and 1 <= p <= 4:
                    low_groups(dve, G_Y, act1_hi, act1_lo, 0, lambda k: vec_col[:, 32 + k:33 + k], None,
                               range(2 * p - 2, 2 * p))
                if p == 5:
                    diagonal(i * 2, i * 4 + 32)
                if p == 6:
                    diagonal(i * 2 + 1, i * 4 + 80)

            stream(p_br, merge, br_after)
            pending[0]()
            merged_low = lambda ms: low_groups(dve, G_M, act1_hi, act1_lo, 0, None, None, ms)
            merged_low(range(2))

            def low_ahead(low_of, i, p):
                if isinstance(i, int) and i == 0 and p < 3:
                    low_of(range(2 * p + 2, 2 * p + 4))

            def residual(i):
                if isinstance(i, int) and i == 0:
                    dve.wait_ge(xres_in, 16)
                    dve.wait_ge(gt_ready, 8)
                else:
                    dve.wait_ge(o_ev, i * 1)
                for t in range(2):
                    wait_bank(dve, p_o, i, t)
                    nc.vector.tensor_tensor(tmp[:, t, :, :].rearrange("p a b -> p (a b)"), PS[:, t, :],
                                            gt1[:, bass.ts(i, NB)], ALU.mult).then_inc(bank_free, 1)
                dve.wait_ge(bank_free, lin(p_o.bank0, i) + 2)
                nc.vector.tensor_tensor(xres[:, :, bass.ts(i, NB)], xres[:, :, bass.ts(i, NB)],
                                        tmp[:, :, :, :].rearrange("p t a b -> p t (a b)"), ALU.add).then_inc(o_ev, 1)

            pending[0] = lambda: None
            stream(p_o, residual, lambda i, p, last: low_ahead(merged_low, i, p))
            pending[0]()
            dve.wait_ge(n_sqrt, 2)
            nc.vector.reciprocal(stat[:, 10:12], stat[:, 10:12]).then_inc(n_rec, 1)
            dve.wait_ge(n_rec, 2)
            dve.wait_ge(tp_done, G_H2)
            for t in range(2):
                nc.vector.tensor_scalar(wide[:, t, :], xres[:, t, :], stat[:, 10 + t:11 + t], None,
                                        ALU.mult).then_inc(n_mul, 1)
            dve.wait_ge(s2_ready, 1)
            dve.wait_ge(xm_out, 16)
            input_low = lambda ms: low_groups(dve, G_H2, act2_hi, act2_lo, H2, lambda k: s2[:, k:k + 1],
                                              lambda k: mod[:, 48 + k, 0:1], ms)
            input_low(range(2))

            def hidden(i):
                for t in range(2):
                    wait_bank(dve, p_f1, i, 2 + t)
                    dve.wait_ge(bank_free, lin(p_f1.bank0, i) + 2)
                    nc.vector.tensor_tensor(stage[:, t, :], stage[:, t, :], PS[:, 2 + t, :], ALU.mult).then_inc(bank_free, 1)

            def hidden_low(i):
                dve.wait_ge(f_hi, i + 1)
                nc.vector.tensor_tensor(
                    act2_lo[:, bass.ds(i * 4, 4), :].rearrange("p (b k) t -> p b (k t)", b=2), PS[:, 4:6, :],
                    act2_hi[:, bass.ds(i * 4, 4), :].bitcast(F32).rearrange("p (b k) t -> p b (k t)", b=2),
                    ALU.subtract).then_inc(f_lo, 1)

            def f1_after(i, p, last):
                low_ahead(input_low, i, p)
                if p == 2 and not (isinstance(i, int) and i == 0):
                    hidden_low(i - 1)

            pending[0] = lambda: None
            stream(p_f1, hidden, f1_after)
            pending[0] = lambda: (hidden(p_f1.n - 1), hidden_low(p_f1.n - 1))

            def finish(i):
                dve.wait_ge(f2_in, i * 32 + 32)
                if not (isinstance(i, int) and i == 0):
                    dve.wait_ge(f2_out, i * 16)
                for t in range(2):
                    wait_bank(dve, p_f2, i, t)
                    nc.vector.tensor_tensor(stage[:, 2 + t, :], PS[:, t, :], tmp[:, 0, :, :].rearrange("p a b -> p (a b)"),
                                            ALU.mult).then_inc(bank_free, 1)
                dve.wait_ge(bank_free, lin(p_f2.bank0, i) + 2)
                nc.vector.tensor_tensor(stage[:, 2:4, :], stage[:, 2:4, :], stage[:, 0:2, :], ALU.add).then_inc(f2_ev, 1)

            stream(p_f2, finish)
            pending[0]()


SETUP = 15
D_A = 8
D_END = D_A + 5
NAMES = ["x", "c", "ctx", "c_ctx", "w_mod", "b_mod", "norm1", "w_in", "conv_w", "conv_b", "dt_bias", "a_log",
         "d_skip", "ssm_norm", "q_norm", "k_norm", "w_ssm_br", "w_attn_br", "w_o", "norm2", "w_ffn_in", "w_ffn_out"]


def shape_constants():
    pos = np.arange(T)
    n = AD // 4
    inv = np.power(np.float32(THETA), -np.arange(n, dtype=np.float32) / np.float32(n)).astype(np.float32)
    ang = np.stack([(pos // GRID_W).astype(np.float32)[:, None] * inv,
                    (pos % GRID_W).astype(np.float32)[:, None] * inv], axis=1)
    cos, sin = np.cos(ang).astype(np.float32), np.sin(ang).astype(np.float32)
    return {
        "c_ident": np.eye(P, dtype=np.float32),
        "c_tri_f": np.triu(np.ones((P, P), np.float32)),
        "c_tri_b": np.tril(np.ones((P, P), np.float32)),
        "rope_cos": np.ascontiguousarray(np.stack([cos, cos], axis=2).reshape(T, AD)),
        "rope_sin": np.ascontiguousarray(np.stack([-sin, sin], axis=2).reshape(T, AD)),
    }


def kernel(**inputs):
    import concourse.bacc as bacc
    from concourse.bass_utils import run_bass_kernel_spmd

    nc = bacc.Bacc("TRN2", target_bir_lowering=False, num_devices=1)
    arrays, aps = {}, {}
    for name, value in [(n, inputs[n]) for n in NAMES] + list(shape_constants().items()):
        value = np.ascontiguousarray(value)
        arrays[f"in_{name}"] = value
        aps[name] = nc.dram_tensor(f"in_{name}", value.shape, mybir.dt.from_np(value.dtype), kind="ExternalInput").ap()
    out = nc.dram_tensor("out_x", (1, T, D), F32, kind="ExternalOutput").ap()
    hybrid_block(nc, aps, out)
    r = run_bass_kernel_spmd(nc, [arrays], core_ids=[0])
    return r.results[0]["out_x"]
```
